# Optimizing a Trainium2 kernel written in Bass

```python
import functools
import jax, jax.numpy as jnp
from jax import lax
import numpy as np

D_MODEL = 2048
BATCH = 1
SEQ = 256
DEPTH = 1
DEC_BATCH = 8
DEC_SEQ = 8
PAST_LEN = 1024
PAGE_SIZE = 128

N_HEADS = 16
QK_NOPE = 128
QK_ROPE = 64
QK_DIM = QK_NOPE + QK_ROPE
V_DIM = 128
KV_LORA = 512
ROPE_BASE = 10000.0
ATTN_SCALE = QK_DIM ** -0.5
Q_BLOCK = 128
POOL_WINDOWS = (2, 4, 8, 16)
N_POOL_GROUPS = len(POOL_WINDOWS)
POOL_WIDTH = D_MODEL // 2
POOL_GROUP = POOL_WIDTH // N_POOL_GROUPS
POOL_BUF = max(POOL_WINDOWS) - 1
D_FF = 5632
CONV_W = 3
EPS = 1e-6
Q_COLS = N_HEADS * QK_DIM
N_BRANCHES = 2
SPLITS = (Q_COLS, Q_COLS + KV_LORA, Q_COLS + KV_LORA + QK_ROPE, Q_COLS + KV_LORA + QK_ROPE + POOL_WIDTH)
IN_WIDTH = SPLITS[-1] + N_BRANCHES * D_MODEL

kernel_name = 'mla_pool_gated_hybrid_step'

def rmsnorm(x, g):
    xf = x.astype(jnp.float32)
    y = xf * lax.rsqrt(jnp.mean(xf * xf, axis=-1, keepdims=True) + EPS)
    return (y * g.astype(jnp.float32)).astype(x.dtype)

def rope(x, pos):
    half = QK_ROPE // 2
    inv = ROPE_BASE ** (-jnp.arange(half, dtype=jnp.float32) / half)
    ang = pos[:, None] * inv[None, :]
    shape = (1, pos.shape[0]) + (1,) * (x.ndim - 3) + (half,)
    c = jnp.cos(ang).reshape(shape)
    s = jnp.sin(ang).reshape(shape)
    xf = x.astype(jnp.float32)
    x1, x2 = xf[..., :half], xf[..., half:]
    return jnp.concatenate([x1 * c - x2 * s, x1 * s + x2 * c], axis=-1).astype(x.dtype)

def mla_prompt(q_nope, q_rope, c_kv, k_rope, w_uk, w_uv):
    B, S = q_nope.shape[:2]
    k_nope = jnp.einsum('bsr,rhd->bshd', c_kv, w_uk)
    v = jnp.einsum('bsr,rhd->bshd', c_kv, w_uv)
    nb = S // Q_BLOCK
    qn_b = q_nope.reshape(B, nb, Q_BLOCK, N_HEADS, QK_NOPE).transpose(1, 0, 2, 3, 4)
    qr_b = q_rope.reshape(B, nb, Q_BLOCK, N_HEADS, QK_ROPE).transpose(1, 0, 2, 3, 4)
    kpos = jnp.arange(S)

    def one_block(args):
        i, qn, qr = args
        s = (jnp.einsum('bqhd,bkhd->bhqk', qn, k_nope)
             + jnp.einsum('bqhr,bkr->bhqk', qr, k_rope)).astype(jnp.float32) * ATTN_SCALE
        qpos = i * Q_BLOCK + jnp.arange(Q_BLOCK)
        mask = kpos[None, :] <= qpos[:, None]
        s = jnp.where(mask[None, None], s, -jnp.inf)
        p = jax.nn.softmax(s, axis=-1).astype(v.dtype)
        return jnp.einsum('bhqk,bkhd->bqhd', p, v)

    o = lax.map(one_block, (jnp.arange(nb), qn_b, qr_b))
    return o.transpose(1, 0, 2, 3, 4).reshape(B, S, N_HEADS, V_DIM)

def mla_sample(q_nope, q_rope, c_new, kr_new, w_uk, w_uv, cache_c, cache_kr, page_table):
    T = q_nope.shape[1]
    n_past = page_table.shape[1] * PAGE_SIZE
    lpos = jnp.arange(n_past + T)
    tpos = n_past + jnp.arange(T)
    mask = lpos[None, :] <= tpos[:, None]

    def one_seq(args):
        qn, qr, cn, krn, pages = args
        c_all = jnp.concatenate([cache_c[pages].reshape(n_past, KV_LORA), cn.astype(cache_c.dtype)], axis=0)
        kr_all = jnp.concatenate([cache_kr[pages].reshape(n_past, QK_ROPE), krn.astype(cache_kr.dtype)], axis=0)
        q_lat = jnp.einsum('thd,rhd->thr', qn, w_uk)
        s = (jnp.einsum('thr,lr->htl', q_lat, c_all)
             + jnp.einsum('thr,lr->htl', qr, kr_all)).astype(jnp.float32) * ATTN_SCALE
        s = jnp.where(mask[None], s, -jnp.inf)
        p = jax.nn.softmax(s, axis=-1).astype(c_all.dtype)
        o_lat = jnp.einsum('htl,lr->thr', p, c_all)
        return jnp.einsum('thr,rhd->thd', o_lat, w_uv)

    return lax.map(one_seq, (q_nope, q_rope, c_new, kr_new, page_table))

def pool_mix(u, buf, pos0, w_pool_group, pool_scale):
    B, T, C = u.shape
    ext = jnp.concatenate([buf.astype(u.dtype), u], axis=1)
    cs = jnp.cumsum(ext.astype(jnp.float32), axis=1)
    cs = jnp.concatenate([jnp.zeros((B, 1, C), jnp.float32), cs], axis=1)
    end = cs[:, POOL_BUF + 1:]
    pos = pos0 + jnp.arange(T, dtype=jnp.float32)
    outs = []
    for g, w in enumerate(POOL_WINDOWS):
        sl = slice(g * POOL_GROUP, (g + 1) * POOL_GROUP)
        start = cs[:, POOL_BUF + 1 - w: POOL_BUF + 1 - w + T, sl]
        cnt = jnp.minimum(pos + 1.0, float(w))[None, :, None]
        outs.append((end[..., sl] - start) / cnt - u[..., sl].astype(jnp.float32))
    pooled = jnp.stack(outs, axis=2).astype(u.dtype)
    y = jnp.einsum('btgc,gcd->btgd', pooled, w_pool_group).reshape(B, T, C) * pool_scale
    return y, ext[:, -POOL_BUF:]

def conv_ffn(h, buf, w_up, conv_w, conv_b, w_down):
    T = h.shape[1]
    z = h @ w_up
    a, v = z[..., :D_FF], z[..., D_FF:]
    ext = jnp.concatenate([buf.astype(a.dtype), a], axis=1)
    conv = conv_b
    for k in range(CONV_W):
        conv = conv + conv_w[k] * ext[:, k:k + T]
    hid = jax.nn.silu(conv) * v
    return hid @ w_down, ext[:, -(CONV_W - 1):]

def trunk_layer(x, pos0, attend, pool_buf, conv_buf, norm_attn_g, w_in, b_gates, kv_norm_g, w_uk, w_uv,
                w_attn_out, w_pool_group, pool_scale, w_pool_out, w_o, norm_ffn_g, w_up, conv_w, conv_b, w_down):
    B, S, _ = x.shape
    h = rmsnorm(x, norm_attn_g)
    z = h @ w_in
    q, c_kv, k_rope, u_pool, z_gate = jnp.split(z, SPLITS, axis=-1)
    pos = pos0 + jnp.arange(S, dtype=jnp.float32)
    q = q.reshape(B, S, N_HEADS, QK_DIM)
    q_nope = q[..., :QK_NOPE]
    q_rope = rope(q[..., QK_NOPE:], pos)
    c_kv = rmsnorm(c_kv, kv_norm_g)
    k_rope = rope(k_rope, pos)
    o_attn = attend(q_nope, q_rope, c_kv, k_rope, w_uk, w_uv).reshape(B, S, N_HEADS * V_DIM)
    o_pool, new_pool = pool_mix(u_pool, pool_buf, pos0, w_pool_group, pool_scale)
    gates = jax.nn.sigmoid((z_gate.reshape(B, S, N_BRANCHES, D_MODEL) + b_gates).astype(jnp.float32)).astype(x.dtype)
    merged = gates[:, :, 0] * (o_attn @ w_attn_out) + gates[:, :, 1] * (o_pool @ w_pool_out)
    x = x + merged @ w_o
    f, new_conv = conv_ffn(rmsnorm(x, norm_ffn_g), conv_buf, w_up, conv_w, conv_b, w_down)
    x = x + f
    return x, c_kv, k_rope, new_pool, new_conv

def setup_inputs(seed: int = 0) -> dict:
    key = jax.random.key(seed)
    ks = jax.random.split(key, 32)
    f32 = jnp.float32

    def nrm(k, shape, scale):
        return jax.random.normal(k, shape, f32) * scale

    n_pages = PAST_LEN // PAGE_SIZE
    n_used = DEC_BATCH * n_pages
    n_phys = (n_used * 5) // 4
    page_table = jax.random.permutation(ks[0], n_phys)[:n_used].reshape(DEC_BATCH, n_pages).astype(jnp.int32)
    L = DEPTH
    return {
        'x_prompt': nrm(ks[1], (BATCH, SEQ, D_MODEL), 1.0),
        'x_sample': nrm(ks[2], (DEC_BATCH, DEC_SEQ, D_MODEL), 1.0),
        'cache_kv_latent': nrm(ks[3], (L, n_phys, PAGE_SIZE, KV_LORA), 1.0),
        'cache_k_rope': nrm(ks[4], (L, n_phys, PAGE_SIZE, QK_ROPE), 1.0),
        'page_table': page_table,
        'state_pool': nrm(ks[5], (L, DEC_BATCH, POOL_BUF, POOL_WIDTH), 1.0),
        'state_conv': nrm(ks[6], (L, DEC_BATCH, CONV_W - 1, D_FF), 1.0),
        'norm_attn_g': 1.0 + nrm(ks[7], (L, D_MODEL), 0.02),
        'w_in': nrm(ks[8], (L, D_MODEL, IN_WIDTH), D_MODEL ** -0.5),
        'b_gates': nrm(ks[9], (L, N_BRANCHES, D_MODEL), 0.02),
        'kv_norm_g': 1.0 + nrm(ks[10], (L, KV_LORA), 0.02),
        'w_uk': nrm(ks[11], (L, KV_LORA, N_HEADS, QK_NOPE), KV_LORA ** -0.5),
        'w_uv': nrm(ks[12], (L, KV_LORA, N_HEADS, V_DIM), KV_LORA ** -0.5),
        'w_attn_out': nrm(ks[13], (L, N_HEADS * V_DIM, D_MODEL), (N_HEADS * V_DIM) ** -0.5),
        'w_pool_group': nrm(ks[14], (L, N_POOL_GROUPS, POOL_GROUP, POOL_GROUP), POOL_GROUP ** -0.5),
        'pool_scale': 1.0 + nrm(ks[15], (L, POOL_WIDTH), 0.02),
        'w_pool_out': nrm(ks[16], (L, POOL_WIDTH, D_MODEL), POOL_WIDTH ** -0.5),
        'w_o': nrm(ks[17], (L, D_MODEL, D_MODEL), D_MODEL ** -0.5),
        'norm_ffn_g': 1.0 + nrm(ks[18], (L, D_MODEL), 0.02),
        'w_up': nrm(ks[19], (L, D_MODEL, 2 * D_FF), D_MODEL ** -0.5),
        'conv_w': nrm(ks[20], (L, CONV_W, D_FF), CONV_W ** -0.5),
        'conv_b': nrm(ks[21], (L, D_FF), 0.02),
        'w_down': nrm(ks[22], (L, D_FF, D_MODEL), D_FF ** -0.5),
        'norm_final_g': 1.0 + nrm(ks[23], (D_MODEL,), 0.02),
    }

def reference(x_prompt, x_sample, cache_kv_latent, cache_k_rope, page_table, state_pool, state_conv,
              norm_attn_g, w_in, b_gates, kv_norm_g, w_uk, w_uv, w_attn_out, w_pool_group, pool_scale,
              w_pool_out, w_o, norm_ffn_g, w_up, conv_w, conv_b, w_down, norm_final_g):
    yp, ys = x_prompt, x_sample
    n_past = page_table.shape[1] * PAGE_SIZE
    kvp, krp, kvs, krs, plp, pls, cvp, cvs = [], [], [], [], [], [], [], []
    for l in range(DEPTH):
        lw = (norm_attn_g[l], w_in[l], b_gates[l], kv_norm_g[l], w_uk[l], w_uv[l], w_attn_out[l],
              w_pool_group[l], pool_scale[l], w_pool_out[l], w_o[l], norm_ffn_g[l], w_up[l], conv_w[l],
              conv_b[l], w_down[l])
        B = yp.shape[0]
        pool0 = jnp.zeros((B, POOL_BUF, POOL_WIDTH), yp.dtype)
        conv0 = jnp.zeros((B, CONV_W - 1, D_FF), yp.dtype)
        yp, c_p, r_p, pool_p, conv_p = trunk_layer(yp, 0, mla_prompt, pool0, conv0, *lw)
        attend_s = functools.partial(mla_sample, cache_c=cache_kv_latent[l], cache_kr=cache_k_rope[l],
                                     page_table=page_table)
        ys, c_s, r_s, pool_s, conv_s = trunk_layer(ys, n_past, attend_s, state_pool[l], state_conv[l], *lw)
        kvp.append(c_p); krp.append(r_p); kvs.append(c_s); krs.append(r_s)
        plp.append(pool_p); pls.append(pool_s); cvp.append(conv_p); cvs.append(conv_s)
    y_prompt = rmsnorm(yp, norm_final_g)
    y_sample = rmsnorm(ys, norm_final_g)
    return (y_prompt, y_sample, jnp.stack(kvp), jnp.stack(krp), jnp.stack(kvs), jnp.stack(krs),
            jnp.stack(plp), jnp.stack(pls), jnp.stack(cvp), jnp.stack(cvs))


_drawn_inputs = setup_inputs


def setup_inputs(seed=0):
    import zlib

    import numpy as np

    out = dict(_drawn_inputs(seed))
    spreads = {}
    factors = {'cache_k_rope': 3.878,
     'norm_attn_g': 2.82,
     'b_gates': 8.0,
     'kv_norm_g': 7.349,
     'pool_scale': 6.017,
     'norm_ffn_g': 8.12,
     'conv_b': 20.312,
     'norm_final_g': 23.846}
    for name, (base, spread) in spreads.items():
        noise = np.random.default_rng([zlib.crc32(name.encode()), seed]).standard_normal(out[name].shape)
        drawn = base * np.exp(spread * noise) if base else spread * noise
        out[name] = __import__('jax').numpy.asarray(drawn.astype(out[name].dtype))
    for name, factor in factors.items():
        out[name] = (out[name] * factor).astype(out[name].dtype)
    return out
```

```python
from contextlib import ExitStack

import concourse.bass as bass
from concourse import mybir

F32 = mybir.dt.float32
F32R = mybir.dt.float32r
I32 = mybir.dt.int32
ACT = mybir.ActivationFunctionType
ALU = mybir.AluOpType
AX = mybir.AxisListType

P = 128
D, NP, NB, NT = 2048, 256, 8, 8
NS = NB * NT
T = NP + NS
KD = D // P
H, DN, DR, DV, R = 16, 128, 64, 128, 512
RT = R // P
PAST, PAGE = 1024, 128
NPG = PAST // PAGE
PW, BUF = 1024, 15
PT_ = PW // P
FF, CW = 5632, 3
FT = FF // P
SCALE = float(DN + DR) ** -0.5
EPS = 1e-6
NEG = -1e30
SLAB = 16 * P
PSEG, SSEG = BUF + NP, BUF + NT
PEXT = PSEG + NB * SSEG
CPS, CSS = CW - 1 + NP, CW - 1 + NT
CEXT = CPS + NB * CSS
FPC = 4
NCH = FT // FPC

ORDER = [("ckv", 4), ("pool", 8), ("krope_group", 2), ("gate_b", 16), ("pool_out", 8), ("gate_a", 16),
         ("q_rope", 8), ("q_nope", 16), ("uk", 4), ("uv", 4), ("ukt", 4), ("uv2", 4), ("attn_out", 16),
         ("w_o", 16), ("ffn", NCH * 12)]
G0 = {}
NSLAB = 0
for _name, _n in ORDER:
    G0[_name] = NSLAB
    NSLAB += _n

VEC = {}
NVEC = 0
for _name, _n in [("g_attn", KD), ("g_kv", RT), ("b_a", KD), ("b_b", KD), ("pool_scale", PT_), ("g_ffn", KD),
                  ("conv_w", CW * FT), ("conv_b", FT), ("g_fin", KD)]:
    VEC[_name] = NVEC
    NVEC += _n
CST = {}
NCST = 0
for _name, _n in [("cos", T), ("sin", T), ("mask", 3 * P), ("mask_new", NT), ("inv_cnt", BUF), ("ident", P),
                  ("ones", P)]:
    CST[_name] = NCST
    NCST += _n


def program(nc, slabs, x, vecs, consts, cache_t, cache_r, cache, pages, pool_hist, conv_hist,
            y, kv_out, kr_out, pool_out, conv_out):
    n_phys = cache.shape[0]
    place = [nc.sbuf_base + (-nc.sbuf_base) % 64]

    def region(nbytes):
        at = place[0]
        place[0] += nbytes + (-nbytes) % 64
        assert place[0] <= nc.sbuf_usable_end, place
        return at

    def sb(name, shape, dt=F32, at=None):
        n = 4
        for d in shape[1:]:
            n *= d
        return nc.alloc_sbuf_tensor_at(name, shape, dt, offset=region(n) if at is None else at)

    with ExitStack() as ctx:
        def sem(name):
            return ctx.enter_context(nc.semaphore(name))

        raw = [sb(f"w_raw{s}", [P, SLAB]) for s in range(2)]
        w_hi = [sb(f"w_hi{s}", [P, SLAB], F32R) for s in range(2)]
        w_lo = [sb(f"w_lo{s}", [P, SLAB], F32R) for s in range(2)]
        vec = sb("vec", [P, NVEC])
        cst = sb("cst", [P, NCST])
        page_sb = sb("page_sb", [1, NB * NPG], I32)
        rstd = sb("rstd", [P, T])
        nv = sb("norm_var", [P, T])
        na = sb("norm_tmp", [P, T])
        nmx = sb("neg_max", [P, 2 * H])
        rsum = sb("row_sum", [P, 2 * H])
        rinv = sb("row_inv", [P, 2 * H])
        smx = sb("sample_max", [P, NB, 12])
        ssum = sb("sample_sum", [P, NB, 4])
        TB = KD * T * 4
        a_reg = region(TB)
        b_reg = region(TB)
        r1 = region(2 * TB)
        qn_reg = region(TB)
        ol_reg = region(TB)
        ch_reg = region(2 * RT * T * 4)
        qr_reg = region(8 * T * 4)
        left = region(5 * 1024)
        gate_a = sb("gate_a", [P, KD, T], at=a_reg)
        m_hi = sb("m_hi", [P, KD, T], F32R, at=a_reg)
        op_hi = sb("op_hi", [P, PT_, T], F32R, at=a_reg)
        op_lo = sb("op_lo", [P, PT_, T], F32R, at=a_reg + TB // 2)
        gate_b = sb("gate_b", [P, KD, T], at=b_reg)
        m_lo = sb("m_lo", [P, KD, T], F32R, at=b_reg)
        uext = sb("uext", [P, PT_, PEXT], at=b_reg)
        hist = sb("hist", [P, PT_ * NB, BUF], at=b_reg + PT_ * PEXT * 4)
        pstate = sb("pstate", [P, PT_, 1 + NB, BUF], at=b_reg + PT_ * PEXT * 4)
        h_hi = sb("h_hi", [P, KD, T], F32R, at=r1)
        h_lo = sb("h_lo", [P, KD, T], F32R, at=r1 + TB)
        kT = sb("kT", [P, H, NP], at=r1)
        vv = sb("vv", [P, 2, H * DV], at=r1 + 16384)
        sm = sb("sm", [P, 3, 3 * P], at=r1 + 32768)
        pt = sb("pt", [P, 2, 3 * P], at=r1 + 32768 + 4608)
        qlat = sb("qlat", [P, NB, RT, P], at=r1)
        ola_lo = sb("ola_lo", [P, NB, RT, P], F32R, at=r1)
        cnew = sb("cnew", [NT, NB, R], at=r1 + 16384)
        ola_hi = sb("ola_hi", [P, NB, RT, P], F32R, at=r1 + 16384)
        ct_ring = sb("ct_ring", [P, 4, R], at=r1 + 32768)
        xT = sb("xT", [P, KD, T], at=qn_reg)
        ta = sb("pool_ta", [P, 2, PEXT], at=qn_reg)
        tb = sb("pool_tb", [P, 2, PEXT], at=qn_reg + 4096)
        pl = sb("pooled", [P, 2, 2, T], at=qn_reg + 8192)
        op32 = sb("op32", [P, 2, T], at=qn_reg + 14336)
        qn = sb("qn", [P, H, T], at=qn_reg)
        o_hi = sb("o_hi", [P, H, T], F32R, at=qn_reg)
        x1 = sb("x1", [P, KD, T], at=qn_reg)
        sq = sb("sq", [P, KD, T], at=ol_reg)
        p_hi = sb("p_hi", [P, PT_, T], F32R, at=ol_reg)
        p_lo = sb("p_lo", [P, PT_, T], F32R, at=ol_reg + TB // 2)
        o_lo = sb("o_lo", [P, H, T], F32R, at=ol_reg)
        x_again = sb("x_again", [P, KD, T], at=ol_reg)
        c32 = sb("c32", [P, RT, T])
        kr = sb("kr", [P, T])
        c_hi = sb("c_hi", [P, RT, T], F32R, at=ch_reg)
        c_lo = sb("c_lo", [P, RT, T], F32R, at=ch_reg + RT * T * 4)
        qs_hi = sb("qs_hi", [P, H, NS], F32R, at=ch_reg)
        qs_lo = sb("qs_lo", [P, H, NS], F32R, at=ch_reg + H * NS * 4)
        c_ring = sb("c_ring", [P, 4, R], at=ch_reg)
        r_ring = sb("r_ring", [DR, 4, PAGE], at=ch_reg + 8192)
        m32 = sb("m32", [P, 2, T], at=ch_reg)
        mt = sb("m_tmp", [P, 2, T], at=ch_reg + 4096)
        qr = sb("qr", [P, 8, T], at=qr_reg)
        sp_ = sb("s_probs", [P, PAST + NT], at=qr_reg)
        spt = sb("s_pt", [P, PAST], at=qr_reg + 4160)
        sptn = sb("s_ptn", [NT, P], at=qr_reg + 4160 + 4096)
        qsw = sb("q_swap", [P, 2, T], at=left)
        qr_s = sb("qr_s", [DR, NB, NT, H], at=left)
        h2_hi = sb("h2_hi", [P, KD, T], F32R, at=r1)
        h2_lo = sb("h2_lo", [P, KD, T], F32R, at=r1 + TB)
        hid_hi = sb("hid_hi", [P, FPC, T], F32R, at=a_reg)
        hid_lo = sb("hid_lo", [P, FPC, T], F32R, at=a_reg + FPC * T * 4)
        aext = sb("aext", [P, 2, CEXT], at=a_reg + 2 * FPC * T * 4)
        cv = sb("cv", [P, 3, CEXT], at=a_reg + 13312)
        silu = sb("silu", [P, 2, CEXT], at=b_reg)
        hid32 = sb("hid32", [P, 2, T], at=b_reg + 4096)
        chist = sb("chist", [P, FT, NB, CW - 1], at=b_reg + 8192)
        cstate = sb("cstate", [P, FT, 1 + NB, CW - 1], at=b_reg + 12288)
        ps = ctx.enter_context(nc.psum_tensor("ps", [P, 8, 512], F32))

        def col(name, i):
            return vec[:, VEC[name] + i:VEC[name] + i + 1]

        def const(name, n=None):
            return cst[:, CST[name]:CST[name] + n]

        ident, ones = const("ident", P), const("ones", P)

        x_in, vec_in, hist_in, again_in, chist_in = (sem(n) for n in
                                                     ("x_in", "vec_in", "hist_in", "again_in", "chist_in"))
        raw_full = [sem("raw_full0"), sem("raw_full1")]
        hi_ready, lo_ready = sem("hi_ready"), sem("lo_ready")
        slab_used, slab_taken = sem("slab_used"), sem("slab_taken")
        sq_done, sum_done, norm, h_32, h_hi_r, h_lo_r = ([sem(f"{n}{i}") for i in range(4)] for n in
                                                         ("sq_done", "sum_done", "norm", "h_32", "h_hi_r", "h_lo_r"))
        u_zero, u_hist, st_done = sem("u_zero"), sem("u_hist"), sem("st_done")
        pool_step, pooled_r, pool_hi, pool_lo = (sem(n) for n in ("pool_step", "pooled_r", "pool_hi", "pool_lo"))
        op_32, op_hi_r, op_lo_r = sem("op_32"), sem("op_hi_r"), sem("op_lo_r")
        kr_copied, kr_step, kr_ready = sem("kr_copied"), sem("kr_step"), sem("kr_ready")
        qr_copied, qr_step, qr_ready = sem("qr_copied"), sem("qr_step"), sem("qr_ready")
        sc_done, sc_masked, mx_done, ex_done, rc_done, pn_done, pt_done, pt_taken, pv_done, ohi_done, olo_done = (
            sem("p_" + n) for n in ("sc_done", "sc_masked", "mx_done", "ex_done", "rc_done", "pn_done", "pt_done",
                                    "pt_taken", "pv_done", "ohi_done", "olo_done"))
        qs_hi_r, qs_lo_r, qrs_ready, cn_done, cn_taken = (sem(n) for n in
                                                          ("qs_hi_r", "qs_lo_r", "qrs_ready", "cn_done", "cn_taken"))
        ct_full = [sem(f"ct_full{i}") for i in range(4)]
        cr_full = [sem(f"cr_full{i}") for i in range(4)]
        cc_full = [sem(f"cc_full{i}") for i in range(4)]
        ct_used, cc_used = sem("ct_used"), sem("cc_used")
        ss_done, sn_done, sx_step, sx_done, sr_step, spn_done, spt_done, spt_taken, spv_done, slh, sll = (
            sem("s_" + n) for n in ("ss_done", "sn_done", "sx_step", "sx_done", "sr_step", "spn_done", "spt_done",
                                    "spt_taken", "spv_done", "slh", "sll"))
        om_hi = sem("om_hi")
        mg_step, mg_32, mg_hi, mg_lo = sem("mg_step"), sem("mg_32"), sem("mg_hi"), sem("mg_lo")
        ah_ready, a_ready, cv_step, silu_r, hd_32, hd_hi, hd_lo = (
            sem("f_" + n) for n in ("ah_ready", "a_ready", "cv_step", "silu_r", "hd_32",
                                    "hd_hi", "hd_lo"))
        a_zero, cs_done, dn_done, dn_taken = sem("f_a_zero"), sem("f_cs_done"), sem("f_dn_done"), sem("f_dn_taken")
        y_step, out_sem = sem("y_step"), sem("out_sem")

        uses = []
        for b in range(NB + 1):
            if b < NB:
                uses += [("t", b * NPG + g) for g in range(NPG)]
            if b:
                uses += [("c", (b - 1) * NPG + g) for g in range(NPG)]
        when = {u: i for i, u in enumerate(uses)}
        loads = sorted(uses, key=lambda u: (when.get((u[0], u[1] - 4), -1), when[u]))

        block = ctx.enter_context(nc.Block())

        @block.sync
        def _(sp):
            sp.dma_start(xT[:, :, :], x).then_inc(x_in, 16)
            sp.dma_start(raw[0][:, :], slabs[0]).then_inc(raw_full[0], 16)
            sp.dma_start(vec[:, :], vecs).then_inc(vec_in, 16)
            sp.dma_start(cst[:, :], consts).then_inc(vec_in, 16)
            sp.dma_start(page_sb[:, :], pages).then_inc(vec_in, 16)
            sp.dma_start(raw[1][:, :], slabs[1]).then_inc(raw_full[1], 16)
            sp.dma_start(hist[:, :, :], pool_hist).then_inc(hist_in, 16)

            def stream(g0, g1):
                with sp.Fori(g0 // 2, g1 // 2) as i:
                    for s in range(2):
                        sp.wait_ge(lo_ready, i * 2 + (s - 1))
                        sp.dma_start(raw[s][:, :], slabs[i * 2 + s]).then_inc(raw_full[s], 16)

            stream(2, G0["uv2"] + 2)

            for kind, n in loads:
                slot = n % 4
                page = sp.value_load(page_sb[0:1, n:n + 1], min_val=0, max_val=n_phys - 1)
                if kind == "t":
                    if n >= 4:
                        sp.wait_ge(ct_used, n - 3)
                    elif n == 0:
                        sp.wait_ge(pt_taken, H)
                        sp.wait_ge(pv_done, H)
                        sp.wait_ge(slab_used, G0["uv2"])
                    sp.dma_start(ct_ring[:, slot, :], cache_t[bass.ds(page, 1)].rearrange("a p c -> (a p) c")
                                 ).then_inc(ct_full[slot], 16)
                    sp.dma_start(r_ring[:, slot, :], cache_r[bass.ds(page, 1)].rearrange("a p c -> (a p) c")
                                 ).then_inc(cr_full[slot], 16)
                else:
                    if n >= 4:
                        sp.wait_ge(cc_used, n - 3)
                    sp.dma_start(c_ring[:, slot, :], cache[bass.ds(page, 1)].rearrange("a p c -> (a p) c")
                                 ).then_inc(cc_full[slot], 16)

            stream(G0["uv2"] + 2, NSLAB)
            sp.wait_ge(cs_done, 2 * FT)
            sp.dma_start(conv_out, cstate[:, :, :, :]).then_inc(out_sem, 16)
            for k in range(4):
                sp.wait_ge(y_step, 4 * (k + 1))
                sp.dma_start(y[:, 4 * k:4 * k + 4, :], x1[:, 4 * k:4 * k + 4, :]).then_inc(out_sem, 16)
            sp.wait_ge(st_done, 16)
            sp.wait_ge(out_sem, 16 * 7)

        @block.gpsimd
        def _(pool):
            pool.wait_ge(hist_in, 16)
            sample = uext[:, :, PSEG:].rearrange("p a (b t) -> p a b t", b=NB)
            hv = hist[:, :, :].rearrange("p (a b) t -> p a b t", a=PT_)
            nc.gpsimd.memset(uext[:, :, 0:BUF], 0.0).then_inc(u_zero, 1)
            for a in range(PT_):
                last = nc.gpsimd.tensor_copy(sample[:, a, :, 0:BUF], hv[:, a])
                last.then_inc(u_zero, 1)
            pool.wait_ge(u_zero, 1 + PT_)
            pool.wait_ge(slab_taken, G0["krope_group"])
            nc.gpsimd.tensor_copy(pstate[:, :, 0, :], uext[:, :, NP:NP + BUF]).then_inc(u_hist, 1)
            for half in range(2):
                a0 = half * PT_ // 2
                for a in range(a0, a0 + PT_ // 2):
                    last = nc.gpsimd.tensor_copy(pstate[:, a, 1:, :], sample[:, a, :, NT:NT + BUF])
                last.then_inc(u_hist, 1)

            pool.wait_ge(chist_in, 16)
            pool.wait_ge(slab_used, G0["ffn"])
            for s in range(2):
                nc.gpsimd.memset(aext[:, s, 0:CW - 1], 0.0).then_inc(a_zero, 1)
            sa = [aext[:, s, CPS:].rearrange("p (b t) -> p b t", b=NB) for s in range(2)]

            def history(f, s):
                nc.gpsimd.tensor_copy(sa[s][:, :, 0:CW - 1], chist[:, bass.ds(f, 1), :, :].rearrange(
                    "p a b t -> p (a b) t")).then_inc(ah_ready, 1)

            def state(f, s):
                nc.gpsimd.tensor_copy(cstate[:, bass.ds(f, 1), 0, :], aext[:, s:s + 1, NP:CPS]).then_inc(cs_done, 1)
                nc.gpsimd.tensor_copy(cstate[:, bass.ds(f, 1), 1:, :].rearrange("p a b t -> p (a b) t"),
                                      sa[s][:, :, NT:CSS]).then_inc(cs_done, 1)

            for s in range(2):
                history(s, s)
            with pool.Fori(0, FT // 2 - 1) as i:
                for s in range(2):
                    pool.wait_ge(a_ready, i * 2 + (s + 1))
                    state(i * 2 + s, s)
                    pool.wait_ge(cv_step, i * 6 + 3 * (s + 1))
                    history(i * 2 + (s + 2), s)
            for s in range(2):
                pool.wait_ge(a_ready, FT - 1 + s)
                state(FT - 2 + s, s)

        @block.scalar
        def _(act):
            def copy(out, in_):
                return nc.scalar.activation(out, in_, ACT.Copy)

            def split(s, g):
                act.wait_ge(raw_full[s], 16 * (g // 2 + 1))
                copy(w_hi[s][:, :], raw[s][:, :]).then_inc(hi_ready, 1)

            def steps(name, take, last=False):
                g0 = G0[name]
                n = dict(ORDER)[name]
                with act.Fori(0, n // 2) as i:
                    for s in range(2):
                        act.wait_ge(slab_used, i * 2 + (g0 + s + 1))
                        act.wait_ge(raw_full[s], i * 16 + 16 * ((g0 + 2) // 2 + 1))
                        copy(w_hi[s][:, :], raw[s][:, :]).then_inc(hi_ready, 1)
                        take(i, s)

            def split_after(g):
                act.wait_ge(slab_used, g + 1)
                split(g % 2, g + 2)

            def squares(n, src, lo, hi):
                for c in range(lo, hi, 4):
                    nc.scalar.activation(sq[:, c:c + 4, :], src[:, c:c + 4, :], ACT.Square).then_inc(sq_done[n], 1)

            def root(n):
                act.wait_ge(norm[n], 1)
                nc.scalar.activation(rstd[:, :], nv[:, :], ACT.Sqrt).then_inc(norm[n], 1)

            def halves_hi(n, out, src, tiles):
                for k in range(tiles):
                    act.wait_ge(h_32[n], k + 1)
                    copy(out[:, k, :], src[:, k, :]).then_inc(h_hi_r[n], 1)

            act.wait_ge(x_in, 16)
            squares(0, xT, 0, KD)
            split(0, 0)
            root(0)
            split(1, 1)
            halves_hi(0, h_hi, xT, KD)

            for g in range(RT):
                split_after(g)
                copy(c32[:, g, :], ps[:, g % 2, 0:T]).then_inc(slab_taken, 1)
            act.wait_ge(slab_taken, RT)
            act.wait_ge(h_lo_r[0], KD)
            squares(1, c32, 0, RT)

            act.wait_ge(u_zero, 1 + PT_)
            for t in range(PT_):
                g = G0["pool"] + t
                split_after(g)
                copy(uext[:, t, BUF:PSEG], ps[:, g % 2, 0:NP])
                copy(uext[:, t, PSEG:].rearrange("p (b t) -> p b t", b=NB)[:, :, BUF:],
                     ps[:, g % 2, NP:T].rearrange("p (b t) -> p b t", b=NB)).then_inc(slab_taken, 1)
                if t == 1:
                    root(1)
                if t == 2:
                    halves_hi(1, c_hi, c32, RT)
                if t % 2 and t > 1:
                    j = (t - 2) // 2
                    act.wait_ge(pooled_r, j + 1)
                    copy(p_hi[:, 2 * j:2 * j + 2, :], pl[:, j % 2, :, :]).then_inc(pool_hi, 1)

            g = G0["krope_group"]
            split_after(g)
            copy(kr[:, :], ps[:, 0, 0:T]).then_inc(kr_copied, 1)
            for q in range(4):
                last = copy(qsw[32 * q:32 * q + 32, 0, :], ps[32 * (q ^ 1):32 * (q ^ 1) + 32, 0, 0:T])
            last.then_inc(slab_taken, 1)
            act.wait_ge(pooled_r, 4)
            copy(p_hi[:, 6:8, :], pl[:, 1, :, :]).then_inc(pool_hi, 1)
            split_after(g + 1)
            act.wait_ge(norm[1], 7 + RT)
            act.dma_start(kv_out, c32[:, :, :]).then_inc(out_sem, 16)
            act.wait_ge(kr_ready, 1)
            act.dma_start(kr_out, kr[0:DR, :]).then_inc(out_sem, 16)
            act.wait_ge(u_hist, 3)
            act.dma_start(pool_out, pstate[:, :, :, :]).then_inc(st_done, 16)
            for t in range(PT_):
                if t >= 2:
                    act.wait_ge(op_lo_r, t - 1)
                last = nc.scalar.activation(op32[:, t % 2, :], ps[:, t, 0:T], ACT.Copy, scale=col("pool_scale", t))
                last.then_inc(op_32, 1)
                act.wait_ge(op_32, t + 1)
                copy(op_hi[:, t, :], op32[:, t % 2, :]).then_inc(op_hi_r, 1)
            act.wait_ge(st_done, 16)

            def gate(buf, bias):
                def take(i, s):
                    k = i * 2 + s
                    nc.scalar.activation(buf[:, bass.ds(k, 1), :].rearrange("p a t -> p (a t)"), ps[:, s, 0:T],
                                         ACT.Sigmoid, bias=vec[:, bass.ds(i * 2 + (s + VEC[bias]), 1)]
                                         ).then_inc(slab_taken, 1)
                return take

            steps("gate_b", gate(gate_b, "b_b"))
            steps("pool_out", lambda i, s: None)
            act.wait_ge(slab_taken, G0["gate_a"])
            steps("gate_a", gate(gate_a, "b_a"))

            def take_rope(i, s):
                j = i * 2 + s
                act.wait_ge(qr_ready, i * 2 + (s + 1))
                copy(qr[:, bass.ds(j, 1), :].rearrange("p a t -> p (a t)"), ps[:, s, 0:T])
                for q in range(4):
                    last = copy(qsw[32 * q:32 * q + 32, s, :], ps[32 * (q ^ 1):32 * (q ^ 1) + 32, s, 0:T])
                last.then_inc(slab_taken, 1)

            steps("q_rope", take_rope)
            steps("q_nope", lambda i, s: copy(qn[:, bass.ds(i * 2 + s, 1), :].rearrange("p a t -> p (a t)"),
                                              ps[:, s, 0:T]).then_inc(slab_taken, 1))

            for j in range(4):
                g = G0["uk"] + j
                split_after(g)
                for q in range(2):
                    last = copy(kT[:, 4 * j + 2 * q:4 * j + 2 * q + 2, :].rearrange("p a t -> p (a t)"),
                                ps[:, g % 2 + 2 * q, :])
                last.then_inc(slab_taken, 1)
            for j in range(4):
                g = G0["uv"] + j
                split_after(g)
                for q in range(2):
                    last = copy(vv[:, q, j * 512:j * 512 + 512], ps[:, g % 2 + 2 * q, :])
                last.then_inc(slab_taken, 1)
            for h0 in range(0, H, 4):
                last = copy(qs_hi[:, h0:h0 + 4, :], qn[:, h0:h0 + 4, NP:T])
            last.then_inc(qs_hi_r, 1)

            for i in range(H + 3):
                if i < H:
                    act.wait_ge(mx_done, 2 * (i + 1))
                    for q in range(2):
                        c0, c1 = (0, P) if q == 0 else (P, 3 * P)
                        nc.scalar.activation(sm[:, i % 3, c0:c1], sm[:, i % 3, c0:c1], ACT.Exp,
                                             bias=nmx[:, 2 * i + q:2 * i + q + 1],
                                             accum_out=rsum[:, 2 * i + q:2 * i + q + 1]).then_inc(ex_done, 1)
                if 2 <= i < H + 2:
                    h = i - 2
                    act.wait_ge(pt_done, h + 1)
                    if h >= 2:
                        act.wait_ge(pv_done, h - 1)
                    copy(pt[:, h % 2, :], ps[:, 4 + h % 2, 0:3 * P]).then_inc(pt_taken, 1)
                if i >= 3:
                    h = i - 3
                    act.wait_ge(pv_done, h + 1)
                    copy(o_hi[:, h, 0:NP], ps[:, 6 + h % 2, 0:NP]).then_inc(ohi_done, 1)

            act.wait_ge(sc_done, H)
            act.wait_ge(pv_done, H)
            for j in range(4):
                g = G0["ukt"] + j
                split_after(g)
                for hh in range(4):
                    src = ps[:, g % 2 + 2 * (hh // 2), (hh % 2) * 256:(hh % 2) * 256 + 256]
                    last = copy(qlat[:, :, :, :].rearrange("p b j (t h) -> p h j b t", h=H)[:, 4 * j + hh],
                                src.rearrange("p (j b t) -> p j b t", j=RT, b=NB))
                last.then_inc(slab_taken, 1)
            for b in range(NB):
                act.wait_ge(cn_done, b + 1)
                copy(cnew[:, b, :], ps[0:NT, b, :]).then_inc(cn_taken, 1)

            for i in range(NB + 1):
                if i < NB:
                    act.wait_ge(sx_step, 4 * (i + 1))
                    if i:
                        act.wait_ge(spt_done, i)
                    b0 = 2 * (i % 2)
                    nm = smx[:, i, 10:11]
                    nc.scalar.activation(sp_[:, 0:PAST].rearrange("p (a t) -> p a t", a=2), ps[:, b0:b0 + 2, :],
                                         ACT.Exp, bias=nm, scale=SCALE, accum_out=ssum[:, i, 0:1]).then_inc(sx_done, 1)
                    nc.scalar.activation(sp_[:, PAST:PAST + NT], smx[:, i, 1:1 + NT], ACT.Exp, bias=nm,
                                         scale=SCALE, accum_out=ssum[:, i, 1:2]).then_inc(sx_done, 1)
                if i:
                    b = i - 1
                    act.wait_ge(spt_done, b + 1)
                    if b:
                        act.wait_ge(spv_done, b)
                    copy(spt[:, :].rearrange("p (a t) -> p a t", a=2), ps[:, 4:6, :])
                    copy(sptn[:, :], ps[0:NT, 7, P:2 * P]).then_inc(spt_taken, 1)
                    act.wait_ge(spv_done, b + 1)
                    for j in range(RT):
                        last = copy(ola_hi[:, b, j, :].rearrange("p (h t) -> p t h", h=H),
                                    ps[:, 6, j * P:j * P + P].rearrange("p (t h) -> p t h", h=H))
                    last.then_inc(slh, 1)

            for j in range(4):
                g = G0["uv2"] + j
                split_after(g)
                copy(o_hi[:, 4 * j:4 * j + 4, NP:T], ps[:, g % 2, 0:4 * NS].rearrange("p (h t) -> p h t", h=4)
                     ).then_inc(om_hi, 1)

            def take_merged(i, s):
                act.wait_ge(mg_32, i * 2 + (s + 1))
                copy(m_hi[:, bass.ds(i * 2 + s, 1), :].rearrange("p a t -> p (a t)"), m32[:, s, :]).then_inc(mg_hi, 1)

            steps("attn_out", take_merged)
            act.wait_ge(slab_used, G0["w_o"])
            act.dma_start(x_again[:, :, :], x).then_inc(again_in, 16)
            steps("w_o", lambda i, s: None)
            act.wait_ge(slab_used, G0["ffn"])
            act.dma_start(chist[:, :, :, :], conv_hist).then_inc(chist_in, 16)

            act.wait_ge(slab_taken, G0["ffn"])
            squares(2, x1, 0, KD)
            root(2)
            halves_hi(2, h2_hi, sq, KD)

            act.wait_ge(a_zero, 2)

            def chunk(c, last_chunk):
                for l in range(12):
                    s = l % 2
                    g = c * 12 + (G0["ffn"] + l)
                    f = l // 2
                    if l < 8 and s:
                        act.wait_ge(hd_32, c * FPC + (f + 1))
                        copy(hid_hi[:, f, :], hid32[:, f % 2, :]).then_inc(hd_hi, 1)
                    if not (last_chunk and l >= 10):
                        act.wait_ge(slab_used, g + 1)
                        act.wait_ge(raw_full[s], c * 96 + 8 * (G0["ffn"] + l - s + 4))
                        copy(w_hi[s][:, :], raw[s][:, :]).then_inc(hi_ready, 1)
                    if l < 8 and not s:
                        act.wait_ge(ah_ready, c * FPC + (f + 1))
                        bank = 2 * (f % 2)
                        copy(aext[:, f % 2, CW - 1:CPS], ps[:, bank, 0:NP])
                        copy(aext[:, f % 2, CPS:].rearrange("p (b t) -> p b t", b=NB)[:, :, CW - 1:],
                             ps[:, bank, NP:T].rearrange("p (b t) -> p b t", b=NB)).then_inc(a_ready, 1)
                        act.wait_ge(cv_step, c * 3 * FPC + 3 * (f + 1))
                        nc.scalar.activation(silu[:, f % 2, CW - 1:], cv[:, 2, CW - 1:], ACT.Silu,
                                             bias=vec[:, bass.ds(c * FPC + (VEC["conv_b"] + f), 1)]).then_inc(silu_r, 1)

            with act.Fori(0, NCH - 1) as c:
                chunk(c, False)
            chunk(NCH - 1, True)
            act.wait_ge(dn_taken, 16 * (NCH + 1))
            squares(3, x1, 0, KD)
            root(3)

        @block.vector
        def _(dve):
            def tt(out, a, b, op):
                return nc.vector.tensor_tensor(out, a, b, op)

            def lo_of(s):
                tt(w_lo[s][:, :], raw[s][:, :], w_hi[s][:, :], ALU.subtract).then_inc(lo_ready, 1)

            def split(g):
                dve.wait_ge(hi_ready, g + 1)
                lo_of(g % 2)

            def steps(name, take):
                g0 = G0[name]
                with dve.Fori(0, dict(ORDER)[name] // 2) as i:
                    for s in range(2):
                        dve.wait_ge(hi_ready, i * 2 + (g0 + s + 3))
                        lo_of(s)
                        take(i, s)

            def rsqrt(n, width):
                dve.wait_ge(sum_done[n], 1)
                nc.vector.tensor_scalar(nv[:, :], ps[:, 7 if n == 1 else 2, 0:T], 1.0 / width, EPS, ALU.mult,
                                        ALU.add).then_inc(norm[n], 1)
                dve.wait_ge(norm[n], 2)
                nc.vector.reciprocal(rstd[:, :], rstd[:, :]).then_inc(norm[n], 1)
                dve.wait_ge(norm[n], 3)
                tt(na[:, :], rstd[:, :], rstd[:, :], ALU.mult).then_inc(norm[n], 1)
                dve.wait_ge(norm[n], 4)
                tt(na[:, :], na[:, :], nv[:, :], ALU.mult).then_inc(norm[n], 1)
                dve.wait_ge(norm[n], 5)
                nc.vector.tensor_scalar(na[:, :], na[:, :], -0.5, 1.5, ALU.mult, ALU.add).then_inc(norm[n], 1)
                dve.wait_ge(norm[n], 6)
                tt(rstd[:, :], rstd[:, :], na[:, :], ALU.mult).then_inc(norm[n], 1)
                dve.wait_ge(norm[n], 7)

            def normed(n, out, src, gain, tiles, done):
                for k in range(tiles):
                    nc.vector.scalar_tensor_tensor(out=out[:, k, :], in0=src[:, k, :], scalar=col(gain, k),
                                                   in1=rstd[:, :], op0=ALU.mult, op1=ALU.mult).then_inc(done, 1)

            def halves_lo(n, lo, src, hi, tiles):
                for k in range(tiles):
                    dve.wait_ge(h_hi_r[n], k + 1)
                    tt(lo[:, k, :], src[:, k, :], hi[:, k, :], ALU.subtract).then_inc(h_lo_r[n], 1)

            split(0)
            dve.wait_ge(vec_in, 48)
            rsqrt(0, D)
            for k in range(KD):
                nc.vector.scalar_tensor_tensor(out=xT[:, k, :], in0=xT[:, k, :], scalar=col("g_attn", k),
                                               in1=rstd[:, :], op0=ALU.mult, op1=ALU.mult).then_inc(h_32[0], 1)
                if k:
                    dve.wait_ge(h_hi_r[0], k)
                    tt(h_lo[:, k - 1, :], xT[:, k - 1, :], h_hi[:, k - 1, :], ALU.subtract).then_inc(h_lo_r[0], 1)
            dve.wait_ge(h_hi_r[0], KD)
            tt(h_lo[:, KD - 1, :], xT[:, KD - 1, :], h_hi[:, KD - 1, :], ALU.subtract).then_inc(h_lo_r[0], 1)
            split(1)
            for g in range(RT):
                split(g + 2)

            n_step = 0

            def pool_group(j):
                nonlocal n_step
                w = 2 << j
                dve.wait_ge(slab_taken, G0["pool"] + 2 * j + 2)
                src = uext[:, 2 * j:2 * j + 2, :]
                cur = src
                for d in range(j + 1):
                    dst = (ta, tb)[d % 2]
                    if n_step:
                        dve.wait_ge(pool_step, n_step)
                    lag = 1 << d
                    first = (2 << d) - 1
                    tt(dst[:, :, first:], cur[:, :, first:], cur[:, :, first - lag:PEXT - lag], ALU.add
                       ).then_inc(pool_step, 1)
                    n_step += 1
                    cur = dst
                dve.wait_ge(pool_step, n_step)
                if j >= 2:
                    dve.wait_ge(pool_lo, j - 1)
                    dve.wait_ge(pool_hi, j - 1)
                out = pl[:, j % 2, :, :]
                for a in range(2):
                    for lo, hi, o in ((BUF + w - 1, PSEG, w - 1),):
                        nc.vector.scalar_tensor_tensor(out=out[:, a, o:NP], in0=cur[:, a, lo:hi], scalar=1.0 / w,
                                                       in1=src[:, a, lo:hi], op0=ALU.mult, op1=ALU.subtract)
                    seg = [z[:, a, PSEG:].rearrange("p (b t) -> p b t", b=NB)[:, :, BUF:] for z in (cur, src)]
                    nc.vector.scalar_tensor_tensor(out=out[:, a, NP:T].rearrange("p (b t) -> p b t", b=NB),
                                                   in0=seg[0], scalar=1.0 / w, in1=seg[1], op0=ALU.mult,
                                                   op1=ALU.subtract)
                    last = tt(out[:, a, 0:w - 1], cur[:, a, BUF:BUF + w - 1], const("inv_cnt", w - 1), ALU.mult)
                last.then_inc(pool_step, 1)
                n_step += 1
                dve.wait_ge(pool_step, n_step)
                for a in range(2):
                    last = tt(out[:, a, 0:w - 1], out[:, a, 0:w - 1], src[:, a, BUF:BUF + w - 1], ALU.subtract)
                last.then_inc(pooled_r, 1)

            def pool_low(j):
                dve.wait_ge(pool_hi, j + 1)
                tt(p_lo[:, 2 * j:2 * j + 2, :], pl[:, j % 2, :, :], p_hi[:, 2 * j:2 * j + 2, :], ALU.subtract
                   ).then_inc(pool_lo, 1)

            for t in range(PT_):
                g = G0["pool"] + t
                split(g + 2)
                if t == 1:
                    rsqrt(1, R)
                    normed(1, c32, c32, "g_kv", RT, h_32[1])
                if t == 2:
                    dve.wait_ge(h_32[1], RT)
                    for k in range(RT):
                        dve.wait_ge(h_hi_r[1], k + 1)
                        tt(c_lo[:, k, :], c32[:, k, :], c_hi[:, k, :], ALU.subtract).then_inc(norm[1], 1)
                if t % 2 == 0 and t:
                    if t >= 4:
                        pool_low(t // 2 - 2)
                    pool_group(t // 2 - 1)
            g = G0["krope_group"]
            split(g + 2)
            pool_low(2)
            pool_group(3)
            dve.wait_ge(slab_taken, g + 1)
            tt(kr[:, :], kr[:, :], const("cos", T), ALU.mult).then_inc(kr_step, 1)
            tt(qsw[:, 0, :], qsw[:, 0, :], const("sin", T), ALU.mult).then_inc(kr_step, 1)
            dve.wait_ge(kr_step, 2)
            tt(kr[:, :], kr[:, :], qsw[:, 0, :], ALU.add).then_inc(kr_ready, 1)
            pool_low(3)
            split(g + 3)
            for t in range(PT_):
                dve.wait_ge(op_hi_r, t + 1)
                last = tt(op_lo[:, t, :], op32[:, t % 2, :], op_hi[:, t, :], ALU.subtract).then_inc(op_lo_r, 1)
            dve.wait_ge(op_lo_r, PT_)
            nc.vector.memset(nmx[:, 0:1], 0.0).then_inc(slab_taken, 1)

            steps("gate_b", lambda i, s: None)
            dve.wait_ge(slab_taken, G0["pool_out"])

            def take_pool_out(i, s):
                dve.wait_ge(slab_used, i * 2 + (G0["pool_out"] + s + 1))
                for j in range(2):
                    g = gate_b[:, bass.ds(i * 4 + (2 * s + j), 1), :].rearrange("p a t -> p (a t)")
                    last = tt(g, ps[:, s + 2 * j, 0:T], g, ALU.mult)
                last.then_inc(slab_taken, 1)

            steps("pool_out", take_pool_out)
            steps("gate_a", lambda i, s: None)
            for s in range(2):
                nc.vector.memset(nmx[:, s:s + 1], 0.0).then_inc(qr_ready, 1)

            def take_rope(i, s):
                dve.wait_ge(slab_taken, i * 2 + (G0["q_rope"] + s + 1))
                t = qr[:, bass.ds(i * 2 + s, 1), :].rearrange("p a t -> p (a t)")
                tt(t, t, const("cos", T), ALU.mult).then_inc(qr_step, 1)
                tt(qsw[:, s, :], qsw[:, s, :], const("sin", T), ALU.mult).then_inc(qr_step, 1)
                dve.wait_ge(qr_step, i * 4 + 2 * (s + 1))
                tt(t, t, qsw[:, s, :], ALU.add).then_inc(qr_ready, 1)

            steps("q_rope", take_rope)
            steps("q_nope", lambda i, s: None)
            for name in ("uk", "uv"):
                for j in range(4):
                    split(G0[name] + j + 2)
            dve.wait_ge(qs_hi_r, 1)
            for h0 in range(0, H, 4):
                last = tt(qs_lo[:, h0:h0 + 4, :], qn[:, h0:h0 + 4, NP:T], qs_hi[:, h0:h0 + 4, :], ALU.subtract)
            last.then_inc(qs_lo_r, 1)
            dve.wait_ge(qr_ready, 2 + 8)
            for odd in range(2):
                for j in range(8):
                    last = nc.vector.tensor_copy(qr_s[:, :, :, 2 * j + odd],
                                                 qr[64 * odd:64 * odd + 64, j, NP:T].rearrange("p (b t) -> p b t", b=NB))
            last.then_inc(qrs_ready, 1)

            for i in range(H + 4):
                if i < H:
                    dve.wait_ge(sc_done, i + 1)
                    if i >= 3:
                        dve.wait_ge(pt_done, i - 2)
                    nc.vector.scalar_tensor_tensor(out=sm[:, i % 3, :], in0=ps[:, 2 + i % 2, 0:3 * P], scalar=SCALE,
                                                   in1=const("mask", 3 * P), op0=ALU.mult, op1=ALU.add
                                                   ).then_inc(sc_masked, 1)
                    dve.wait_ge(sc_masked, i + 1)
                    for q in range(2):
                        c0, c1 = (0, P) if q == 0 else (P, 3 * P)
                        nc.vector.tensor_reduce(nmx[:, 2 * i + q:2 * i + q + 1], sm[:, i % 3, c0:c1], AX.X, ALU.max,
                                                negate=True).then_inc(mx_done, 1)
                if 1 <= i < H + 1:
                    h = i - 1
                    dve.wait_ge(ex_done, 2 * (h + 1))
                    nc.vector.reciprocal(rinv[:, 2 * h:2 * h + 2], rsum[:, 2 * h:2 * h + 2]).then_inc(rc_done, 1)
                    dve.wait_ge(rc_done, h + 1)
                    for q in range(2):
                        c0, c1 = (0, P) if q == 0 else (P, 3 * P)
                        nc.vector.tensor_scalar(sm[:, h % 3, c0:c1], sm[:, h % 3, c0:c1],
                                                rinv[:, 2 * h + q:2 * h + q + 1], None, ALU.mult).then_inc(pn_done, 1)
                if i >= 4:
                    h = i - 4
                    dve.wait_ge(ohi_done, h + 1)
                    tt(o_lo[:, h, 0:NP], ps[:, 6 + h % 2, 0:NP], o_hi[:, h, 0:NP], ALU.subtract).then_inc(olo_done, 1)

            for j in range(4):
                split(G0["ukt"] + j + 2)

            for i in range(NB + 1):
                if i < NB:
                    dve.wait_ge(ss_done, i + 1)
                    tt(smx[:, i, 1:1 + NT], ps[:, 7, 0:NT], const("mask_new", NT), ALU.add).then_inc(sn_done, 1)
                    b0 = 2 * (i % 2)
                    nc.vector.tensor_reduce(smx[:, i, 0:1], ps[:, b0:b0 + 2, :], AX.XY, ALU.max).then_inc(sx_step, 1)
                    dve.wait_ge(sx_step, 4 * i + 1)
                    dve.wait_ge(sn_done, i + 1)
                    nc.vector.tensor_reduce(smx[:, i, 9:10], smx[:, i, 0:1 + NT], AX.X, ALU.max).then_inc(sx_step, 1)
                    dve.wait_ge(sx_step, 4 * i + 2)
                    nc.vector.tensor_scalar(smx[:, i, 10:11], smx[:, i, 9:10], -SCALE, None, ALU.mult
                                            ).then_inc(sx_step, 2)
                    dve.wait_ge(sx_done, 2 * (i + 1))
                    tt(ssum[:, i, 2:3], ssum[:, i, 0:1], ssum[:, i, 1:2], ALU.add).then_inc(sr_step, 1)
                    dve.wait_ge(sr_step, 2 * i + 1)
                    nc.vector.reciprocal(ssum[:, i, 3:4], ssum[:, i, 2:3]).then_inc(sr_step, 1)
                    dve.wait_ge(sr_step, 2 * i + 2)
                    nc.vector.tensor_scalar(sp_[:, :], sp_[:, :], ssum[:, i, 3:4], None, ALU.mult).then_inc(spn_done, 1)
                if i:
                    b = i - 1
                    dve.wait_ge(slh, b + 1)
                    for j in range(RT):
                        last = tt(ola_lo[:, b, j, :].rearrange("p (h t) -> p t h", h=H),
                                  ps[:, 6, j * P:j * P + P].rearrange("p (t h) -> p t h", h=H),
                                  ola_hi[:, b, j, :].rearrange("p (h t) -> p t h", h=H), ALU.subtract)
                    last.then_inc(sll, 1)

            for j in range(4):
                g = G0["uv2"] + j
                split(g + 2)
                dve.wait_ge(om_hi, j + 1)
                tt(o_lo[:, 4 * j:4 * j + 4, NP:T], ps[:, g % 2, 0:4 * NS].rearrange("p (h t) -> p h t", h=4),
                   o_hi[:, 4 * j:4 * j + 4, NP:T], ALU.subtract).then_inc(slab_taken, 1)

            def take_merged(i, s):
                k = i * 2 + s
                dve.wait_ge(slab_used, i * 2 + (G0["attn_out"] + s + 1))
                tt(mt[:, s, :], ps[:, s, 0:T], gate_a[:, bass.ds(k, 1), :].rearrange("p a t -> p (a t)"), ALU.mult
                   ).then_inc(slab_taken, 1)
                dve.wait_ge(slab_taken, i * 2 + (G0["attn_out"] + s + 1))
                tt(m32[:, s, :], mt[:, s, :], gate_b[:, bass.ds(k, 1), :].rearrange("p a t -> p (a t)"), ALU.add
                   ).then_inc(mg_32, 1)
                dve.wait_ge(mg_hi, i * 2 + (s + 1))
                tt(m_lo[:, bass.ds(k, 1), :].rearrange("p a t -> p (a t)"), m32[:, s, :],
                   m_hi[:, bass.ds(k, 1), :].rearrange("p a t -> p (a t)"), ALU.subtract).then_inc(mg_lo, 1)

            steps("attn_out", take_merged)
            dve.wait_ge(again_in, 16)

            def take_o(i, s):
                k = i * 2 + s
                dve.wait_ge(slab_used, i * 2 + (G0["w_o"] + s + 1))
                tt(x1[:, bass.ds(k, 1), :].rearrange("p a t -> p (a t)"), ps[:, s, 0:T],
                   x_again[:, bass.ds(k, 1), :].rearrange("p a t -> p (a t)"), ALU.add).then_inc(slab_taken, 1)

            steps("w_o", take_o)
            rsqrt(2, D)
            for k in range(KD):
                nc.vector.scalar_tensor_tensor(out=sq[:, k, :], in0=x1[:, k, :], scalar=col("g_ffn", k),
                                               in1=rstd[:, :], op0=ALU.mult, op1=ALU.mult).then_inc(h_32[2], 1)
                if k:
                    dve.wait_ge(h_hi_r[2], k)
                    tt(h2_lo[:, k - 1, :], sq[:, k - 1, :], h2_hi[:, k - 1, :], ALU.subtract).then_inc(h_lo_r[2], 1)
            dve.wait_ge(h_hi_r[2], KD)
            tt(h2_lo[:, KD - 1, :], sq[:, KD - 1, :], h2_hi[:, KD - 1, :], ALU.subtract).then_inc(h_lo_r[2], 1)

            nc.vector.memset(nmx[:, 1:2], 0.0).then_inc(dn_taken, 16)

            def chunk(c, last_chunk):
                for l in range(12):
                    s = l % 2
                    f = l // 2
                    g = c * 12 + (G0["ffn"] + l)
                    if l < 8 and s:
                        vb = 2 * (f % 2) + 1
                        dve.wait_ge(slab_used, g + 1)
                        dve.wait_ge(silu_r, c * FPC + (f + 1))
                        nc.vector.tensor_tensor(hid32[:, f % 2, 0:NP], ps[:, vb, 0:NP], silu[:, f % 2, CW - 1:CPS],
                                                ALU.mult)
                        tt(hid32[:, f % 2, NP:T].rearrange("p (b t) -> p b t", b=NB),
                           ps[:, vb, NP:T].rearrange("p (b t) -> p b t", b=NB),
                           silu[:, f % 2, CPS:].rearrange("p (b t) -> p b t", b=NB)[:, :, CW - 1:],
                           ALU.mult).then_inc(hd_32, 1)
                        dve.wait_ge(hd_32, c * FPC + (f + 1))
                        dve.wait_ge(hd_hi, c * FPC + (f + 1))
                        tt(hid_lo[:, f, :], hid32[:, f % 2, :], hid_hi[:, f, :], ALU.subtract).then_inc(hd_lo, 1)
                    if l >= 8:
                        for n in range(4):
                            bank = 4 * (1 - s) + n
                            k = 4 * (l - 8) + n
                            if n < 3:
                                dve.wait_ge(dn_done, c * 12 + (3 * (l - 8) + n + 1))
                            else:
                                dve.wait_ge(slab_used, g + 1)
                            tt(x1[:, k, :], ps[:, bank, 0:T], x1[:, k, :], ALU.add).then_inc(dn_taken, 1)
                    if not (last_chunk and l >= 10):
                        dve.wait_ge(hi_ready, g + 3)
                        lo_of(s)
                    if l < 8 and not s:
                        dve.wait_ge(a_ready, c * FPC + (f + 1))
                        dve.wait_ge(ah_ready, c * FPC + (f + 1))
                        a = aext[:, f % 2, :]
                        for j in range(CW):
                            w = vec[:, bass.ds(c * FPC + (VEC["conv_w"] + j * FT + f), 1)]
                            src = a[:, j:CEXT - (CW - 1 - j)]
                            dst = cv[:, j, CW - 1:]
                            if j == 0:
                                nc.vector.tensor_scalar(dst, src, w, None, ALU.mult).then_inc(cv_step, 1)
                            else:
                                dve.wait_ge(cv_step, c * 3 * FPC + (3 * f + j))
                                nc.vector.scalar_tensor_tensor(out=dst, in0=src, scalar=w, in1=cv[:, j - 1, CW - 1:],
                                                               op0=ALU.mult, op1=ALU.add).then_inc(cv_step, 1)

            with dve.Fori(0, NCH - 1) as c:
                chunk(c, False)
            chunk(NCH - 1, True)
            rsqrt(3, D)
            for k in range(KD):
                nc.vector.scalar_tensor_tensor(out=x1[:, k, :], in0=x1[:, k, :], scalar=col("g_fin", k),
                                               in1=rstd[:, :], op0=ALU.mult, op1=ALU.mult).then_inc(y_step, 1)

        @block.tensor
        def _(pe):
            def mm(out, a, b, start, stop, **kw):
                return nc.tensor.matmul(out, a, b, start=start, stop=stop, **kw)

            def blk(w, n, m=1):
                return w[:, n * P:(n + m) * P]

            def slab(s, g, outs, per_out=False, before=None, free=True):
                pe.wait_ge(hi_ready, g + 1)
                if free:
                    pe.wait_ge(slab_taken, g - 1)
                if per_out:
                    pe.wait_ge(lo_ready, g + 1)

                def high(out, terms):
                    for k, (w, hi, lo) in enumerate(terms):
                        if before is not None:
                            before(k)
                        mm(out, w(w_hi[s]), hi, k == 0, False)
                        mm(out, w(w_hi[s]), lo, False, False)

                def low(out, terms):
                    for k, (w, hi, lo) in enumerate(terms):
                        last = mm(out, w(w_lo[s]), hi, False, k == len(terms) - 1)
                    return last

                if per_out:
                    for out, terms in outs:
                        high(out, terms)
                        last = low(out, terms)
                else:
                    for out, terms in outs:
                        high(out, terms)
                    pe.wait_ge(lo_ready, g + 1)
                    for out, terms in outs:
                        last = low(out, terms)
                last.then_inc(slab_used, 1)

            def wb(n, m=1):
                return lambda w: blk(w, n, m)

            def dense(s, hi, lo):
                return [(ps[:, s, 0:T], [(wb(k), hi[:, k, :], lo[:, k, :]) for k in range(KD)])]

            def group(name, outs_of, **kw):
                g0 = G0[name]
                with pe.Fori(0, dict(ORDER)[name] // 2) as i:
                    for s in range(2):
                        slab(s, i * 2 + (g0 + s), outs_of(s), **kw)

            def sum_squares(n, tiles, bank):
                for k in range(tiles):
                    if k % 4 == 0:
                        pe.wait_ge(sq_done[n], k // 4 + 1)
                    last = mm(ps[:, bank, 0:T], ones, sq[:, k, :], k == 0, k == tiles - 1)
                last.then_inc(sum_done[n], 1)

            pe.wait_ge(vec_in, 48)
            sum_squares(0, KD, 2)

            def wait_h(n):
                def before(k):
                    pe.wait_ge(h_hi_r[n], k + 1)
                    pe.wait_ge(h_lo_r[n], k + 1)
                return before

            slab(0, 0, dense(0, h_hi, h_lo), before=wait_h(0), free=False)
            slab(1, 1, dense(1, h_hi, h_lo), free=False)
            for g in range(2, RT):
                slab(g % 2, g, dense(g % 2, h_hi, h_lo))
            g = G0["pool"]
            slab(0, g, dense(0, h_hi, h_lo))
            sum_squares(1, RT, 7)
            slab(1, g + 1, dense(1, h_hi, h_lo))
            with pe.Fori(1, PT_ // 2) as i:
                for s in range(2):
                    slab(s, i * 2 + (g + s), dense(s, h_hi, h_lo))
            g = G0["krope_group"]
            slab(0, g, dense(0, h_hi, h_lo))
            pe.wait_ge(slab_taken, g + 1)
            pe.wait_ge(norm[1], 1)
            pe.wait_ge(pool_hi, 4)
            pe.wait_ge(pool_lo, 4)
            slab(1, g + 1, [(ps[:, t, 0:T], [(wb(2 * t + k), p_hi[:, 2 * (t // 2) + k, :], p_lo[:, 2 * (t // 2) + k, :])
                                             for k in range(2)]) for t in range(PT_)])
            pe.wait_ge(slab_taken, g + 2)
            group("gate_b", lambda s: dense(s, h_hi, h_lo))
            group("pool_out", lambda s: [(ps[:, s + 2 * j, 0:T], [(wb(8 * j + k), op_hi[:, k, :], op_lo[:, k, :])
                                                                  for k in range(PT_)]) for j in range(2)])
            for name in ("gate_a", "q_rope", "q_nope"):
                group(name, lambda s: dense(s, h_hi, h_lo))

            for j in range(4):
                g = G0["uk"] + j
                slab(g % 2, g, [(ps[:, g % 2 + 2 * (hh // 2), (hh % 2) * NP:(hh % 2) * NP + NP],
                                 [(wb(4 * hh + r), c_hi[:, r, 0:NP], c_lo[:, r, 0:NP]) for r in range(RT)])
                                for hh in range(4)], per_out=True)
            for j in range(4):
                g = G0["uv"] + j
                s = g % 2
                pe.wait_ge(hi_ready, g + 1)
                pe.wait_ge(lo_ready, g + 1)
                pe.wait_ge(slab_taken, g - 1)
                for q in range(2):
                    for r in range(RT):
                        ch, cl = c_hi[:, r, q * P:q * P + P], c_lo[:, r, q * P:q * P + P]
                        mm(ps[:, s + 2 * q, :], ch, blk(w_hi[s], 4 * r, 4), r == 0, False)
                        mm(ps[:, s + 2 * q, :], cl, blk(w_hi[s], 4 * r, 4), False, False)
                        last = mm(ps[:, s + 2 * q, :], ch, blk(w_lo[s], 4 * r, 4), False, r == RT - 1)
                last.then_inc(slab_used, 1)

            pe.wait_ge(slab_taken, G0["ukt"])
            pe.wait_ge(kr_ready, 1)
            pe.wait_ge(qrs_ready, 1)
            for i in range(H + 3):
                if i < H:
                    if i >= 2:
                        pe.wait_ge(sc_masked, i - 1)
                    r0 = 64 * (i % 2)
                    for q in range(2):
                        out = ps[:, 2 + i % 2, q * P:q * P + (q + 1) * P]
                        mm(out, qn[:, i, q * P:q * P + P], kT[:, i, 0:(q + 1) * P], True, False)
                        last = mm(out, qr[r0:r0 + 64, i // 2, q * P:q * P + P], kr[r0:r0 + 64, 0:(q + 1) * P],
                                  False, True)
                    last.then_inc(sc_done, 1)
                if 2 <= i < H + 2:
                    h = i - 2
                    pe.wait_ge(pn_done, 2 * (h + 1))
                    if h >= 2:
                        pe.wait_ge(pt_taken, h - 1)
                    for q in range(3):
                        last = nc.tensor.transpose(ps[:, 4 + h % 2, q * P:q * P + P], sm[:, h % 3, q * P:q * P + P],
                                                   ident)
                    last.then_inc(pt_done, 1)
                if i >= 3:
                    h = i - 3
                    pe.wait_ge(pt_taken, h + 1)
                    if h >= 2:
                        pe.wait_ge(olo_done, h - 1)
                    out = ps[:, 6 + h % 2, :]
                    mm(out[:, 0:NP], vv[:, 0, h * DV:(h + 1) * DV], pt[:, h % 2, 0:NP], True, False)
                    mm(out[:, P:NP], vv[:, 1, h * DV:(h + 1) * DV], pt[:, h % 2, NP:3 * P], False, True
                       ).then_inc(pv_done, 1)

            pe.wait_ge(qs_lo_r, 1)
            pe.wait_ge(sc_masked, H)
            for j in range(4):
                g = G0["ukt"] + j
                slab(g % 2, g, [(ps[:, g % 2 + 2 * (hh // 2), (hh % 2) * 256 + r * NS:(hh % 2) * 256 + (r + 1) * NS],
                                 [(wb(4 * hh + r), qs_hi[:, 4 * j + hh, :], qs_lo[:, 4 * j + hh, :])])
                                for hh in range(4) for r in range(RT)], per_out=True)
            pe.wait_ge(slab_taken, G0["uv2"])
            pe.wait_ge(olo_done, H)
            for b in range(NB):
                for r in range(RT):
                    last = nc.tensor.transpose(ps[0:NT, b, r * P:r * P + P], c32[:, r, NP + NT * b:NP + NT * (b + 1)],
                                               ident)
                last.then_inc(cn_done, 1)
            pe.wait_ge(cn_taken, NB)

            for i in range(NB + 1):
                if i < NB:
                    if i >= 2:
                        pe.wait_ge(sx_done, 2 * (i - 1))
                    qr_b = qr_s[:, i, :, :].rearrange("p t h -> p (t h)")
                    for pg in range(NPG):
                        n = i * NPG + pg
                        out = ps[:, 2 * (i % 2) + pg // 4, (pg % 4) * PAGE:(pg % 4 + 1) * PAGE]
                        pe.wait_ge(ct_full[n % 4], 16 * (n // 4 + 1))
                        for r in range(RT):
                            mm(out, qlat[:, i, r, :], ct_ring[:, n % 4, r * PAGE:(r + 1) * PAGE], r == 0, False)
                        pe.wait_ge(cr_full[n % 4], 16 * (n // 4 + 1))
                        mm(out, qr_b, r_ring[:, n % 4, :], False, True).then_inc(ct_used, 1)
                    out = ps[:, 7, 0:NT]
                    if i:
                        pe.wait_ge(sn_done, i)
                    if i >= 2:
                        pe.wait_ge(spt_taken, i - 1)
                    t0 = NP + NT * i
                    for r in range(RT):
                        mm(out, qlat[:, i, r, :], c32[:, r, t0:t0 + NT], r == 0, False)
                    mm(out, qr_b, kr[0:DR, t0:t0 + NT], False, True).then_inc(ss_done, 1)
                if i:
                    b = i - 1
                    pe.wait_ge(spn_done, b + 1)
                    if b:
                        pe.wait_ge(spt_taken, b)
                    for pg in range(NPG):
                        nc.tensor.transpose(ps[:, 4 + pg // 4, (pg % 4) * P:(pg % 4 + 1) * P],
                                            sp_[:, pg * P:pg * P + P], ident)
                    pe.wait_ge(sn_done, min(i + 1, NB))
                    nc.tensor.transpose(ps[0:NT, 7, P:2 * P], sp_[:, PAST:PAST + NT], ident).then_inc(spt_done, 1)
                    pe.wait_ge(spt_taken, b + 1)
                    if b:
                        pe.wait_ge(sll, b)
                    for pg in range(NPG):
                        n = b * NPG + pg
                        pe.wait_ge(cc_full[n % 4], 16 * (n // 4 + 1))
                        for r in range(RT):
                            last = mm(ps[:, 6, r * P:r * P + P], c_ring[:, n % 4, r * P:r * P + P],
                                      spt[:, pg * P:pg * P + P], pg == 0 and r == 0, False, skip_group_check=True)
                        last.then_inc(cc_used, 1)
                    for r in range(RT):
                        last = mm(ps[:, 6, r * P:r * P + P], cnew[:, b, r * P:r * P + P], sptn[:, :], False,
                                  r == RT - 1, skip_group_check=True)
                    last.then_inc(spv_done, 1)

            pe.wait_ge(sll, NB)
            for j in range(4):
                g = G0["uv2"] + j
                slab(g % 2, g, [(ps[:, g % 2, hh * NS:(hh + 1) * NS].rearrange("p (b t) -> p b t", b=NB),
                                 [(wb(4 * r + hh), *(z[:, :, r, (4 * j + hh) * NT:(4 * j + hh + 1) * NT]
                                                     for z in (ola_hi, ola_lo))) for r in range(RT)])
                                for hh in range(4)], per_out=True)
            pe.wait_ge(slab_taken, G0["attn_out"])
            group("attn_out", lambda s: dense(s, o_hi, o_lo))
            pe.wait_ge(mg_lo, KD)
            pe.wait_ge(slab_taken, G0["w_o"])
            group("w_o", lambda s: dense(s, m_hi, m_lo))
            sum_squares(2, KD, 2)
            pe.wait_ge(h_hi_r[2], KD)
            pe.wait_ge(h_lo_r[2], KD)
            pe.wait_ge(norm[2], 1)
            pe.wait_ge(dn_taken, 16)

            with pe.Fori(0, NCH) as c:
                for l in range(8):
                    s, f = l % 2, l // 2
                    if s == 0:
                        if f >= 2:
                            pe.wait_ge(a_ready, c * FPC + (f - 1))
                    elif f >= 2:
                        pe.wait_ge(hd_32, c * FPC + (f - 1))
                    if l == 0:
                        pe.wait_ge(dn_taken, c * 16 + 16)
                    slab(s, c * 12 + (G0["ffn"] + l),
                         [(ps[:, 2 * (f % 2) + s, 0:T], [(wb(k), h2_hi[:, k, :], h2_lo[:, k, :]) for k in range(KD)])],
                         free=False)
                for d in range(4):
                    s = d % 2
                    g = c * 12 + (G0["ffn"] + 8 + d)
                    pe.wait_ge(hi_ready, g + 1)
                    pe.wait_ge(lo_ready, g + 1)
                    banks = [4 * (1 - s) + n for n in range(4)]
                    order = ([(n, k) for k in range(FPC) for n in range(4)] if d == 0 else
                             [(n, k) for n in range(4) for k in range(FPC)])
                    for n, k in order:
                        if d == 0 and n == 0:
                            pe.wait_ge(hd_hi, c * FPC + (k + 1))
                            pe.wait_ge(hd_lo, c * FPC + (k + 1))
                        if d >= 2 and k == 0:
                            pe.wait_ge(dn_taken, c * 16 + (16 + 4 * (d - 2) + n + 1))
                        out = ps[:, banks[n], 0:T]
                        w = 4 * n + k
                        mm(out, blk(w_hi[s], w), hid_hi[:, k, :], k == 0, False)
                        mm(out, blk(w_hi[s], w), hid_lo[:, k, :], False, False)
                        last = mm(out, blk(w_lo[s], w), hid_hi[:, k, :], False, k == FPC - 1)
                        if k == FPC - 1:
                            last.then_inc(dn_done if n < 3 else slab_used, 1)
            sum_squares(3, KD, 2)


def _tables():
    import numpy as np

    t = np.zeros((P, NCST), np.float32)
    half = DR // 2
    inv = (np.float32(10000.0) ** (-np.arange(half, dtype=np.float32) / np.float32(half))).astype(np.float32)
    pos = np.concatenate([np.arange(NP), np.tile(PAST + np.arange(NT), NB)]).astype(np.float32)
    ang = (pos[None, :] * inv[:, None]).astype(np.float32).astype(np.float64)
    t[:, CST["cos"]:CST["cos"] + T] = np.tile(np.cos(ang), (4, 1))
    t[:, CST["sin"]:CST["sin"] + T] = np.concatenate([-np.sin(ang), np.sin(ang)] * 2)
    tri = np.where(np.arange(P)[None, :] <= np.arange(P)[:, None], 0.0, NEG)
    t[:, CST["mask"]:CST["mask"] + P] = tri
    t[:, CST["mask"] + 2 * P:CST["mask"] + 3 * P] = tri
    t[:, CST["mask_new"]:CST["mask_new"] + NT] = np.where(np.arange(NT)[None, :] <= (np.arange(P) // H)[:, None],
                                                          0.0, NEG)
    t[:, CST["inv_cnt"]:CST["inv_cnt"] + BUF] = 1.0 / np.arange(1, BUF + 1)
    t[:, CST["ident"]:CST["ident"] + P] = np.eye(P)
    t[:, CST["ones"]:CST["ones"] + P] = 1.0
    return t


def _slabs(w_in, w_uk, w_uv, w_attn_out, w_pool_group, w_pool_out, w_o, w_up, w_down):
    import numpy as np

    out = np.empty((NSLAB, P, 16, P), np.float32)

    def put(name, blocks, off=0):
        g = G0[name] + off
        out[g:g + len(blocks)] = blocks.transpose(0, 2, 1, 3)

    def tiles(w):
        return w.reshape(w.shape[0] // P, P, w.shape[1] // P, P).transpose(2, 0, 1, 3)

    qc = H * (DN + DR)
    q = w_in[:, :qc].reshape(D, H, DN + DR)
    put("q_nope", tiles(q[:, :, :DN].reshape(D, H * DN)))
    put("q_rope", tiles(q[:, :, DN:].reshape(D, H * DR)))
    put("ckv", tiles(w_in[:, qc:qc + R]))
    k = w_in[:, qc + R:qc + R + DR]
    put("krope_group", tiles(np.concatenate([k, k], 1)))
    c = qc + R + DR
    put("pool", tiles(w_in[:, c:c + PW]))
    put("gate_a", tiles(w_in[:, c + PW:c + PW + D]))
    put("gate_b", tiles(w_in[:, c + PW + D:]))
    g = w_pool_group.reshape(4, 2, P, 2, P).transpose(0, 3, 1, 2, 4)
    put("krope_group", g.reshape(1, 16, P, P), 1)
    put("pool_out", tiles(w_pool_out).reshape(8, 16, P, P))
    uk = w_uk.reshape(RT, P, 4, 4, DN)
    put("uk", uk.transpose(2, 3, 0, 1, 4).reshape(4, 16, P, P))
    put("ukt", uk.transpose(2, 3, 0, 4, 1).reshape(4, 16, P, P))
    uv = w_uv.reshape(RT, P, 4, 4, DV).transpose(2, 0, 3, 1, 4).reshape(4, 16, P, P)
    put("uv", uv)
    put("uv2", uv)
    put("attn_out", tiles(w_attn_out))
    put("w_o", tiles(w_o))
    up = tiles(w_up).reshape(2, NCH, FPC, KD, P, P).transpose(1, 2, 0, 3, 4, 5).reshape(NCH, 8, 16, P, P)
    down = w_down.reshape(NCH, FPC, P, 4, 4, P).transpose(0, 3, 4, 1, 2, 5).reshape(NCH, 4, 16, P, P)
    put("ffn", np.concatenate([up, down], 1).reshape(NCH * 12, 16, P, P))
    return out.reshape(NSLAB, P, SLAB)


def kernel(x_prompt, x_sample, cache_kv_latent, cache_k_rope, page_table, state_pool, state_conv, norm_attn_g, w_in,
           b_gates, kv_norm_g, w_uk, w_uv, w_attn_out, w_pool_group, pool_scale, w_pool_out, w_o, norm_ffn_g, w_up,
           conv_w, conv_b, w_down, norm_final_g):
    import numpy as np
    import concourse.bacc as bacc
    from concourse.bass_utils import run_bass_kernel_spmd as run

    def arr(a):
        return np.asarray(a)

    def cols(*vs):
        return np.concatenate([arr(v).reshape(-1, P).T for v in vs], 1)

    nc = bacc.Bacc("TRN2", target_bir_lowering=False, num_devices=1, dynamic_dma_scratch_size=1024)
    xx = np.concatenate([arr(x_prompt).reshape(NP, D), arr(x_sample).reshape(NS, D)])
    cache = arr(cache_kv_latent)[0]
    ins = {
        "slabs": _slabs(arr(w_in)[0], arr(w_uk)[0], arr(w_uv)[0], arr(w_attn_out)[0], arr(w_pool_group)[0],
                        arr(w_pool_out)[0], arr(w_o)[0], arr(w_up)[0], arr(w_down)[0]),
        "x": xx.T.reshape(KD, P, T).transpose(1, 0, 2),
        "vecs": cols(norm_attn_g, kv_norm_g, arr(b_gates)[0, 0], arr(b_gates)[0, 1], pool_scale, norm_ffn_g,
                     conv_w, conv_b, norm_final_g),
        "consts": _tables(),
        "cache_t": cache.reshape(-1, PAGE, RT, P).transpose(0, 3, 2, 1).reshape(-1, P, RT * PAGE),
        "cache_r": arr(cache_k_rope)[0].transpose(0, 2, 1),
        "cache": cache,
        "pages": arr(page_table).reshape(1, -1),
        "pool_hist": arr(state_pool)[0].reshape(NB, BUF, PT_, P).transpose(3, 2, 0, 1).reshape(P, PT_ * NB, BUF),
        "conv_hist": arr(state_conv)[0].reshape(NB, CW - 1, FT, P).transpose(3, 2, 0, 1),
    }
    ins = {n: np.ascontiguousarray(a) for n, a in ins.items()}
    aps = [nc.dram_tensor("in_" + n, a.shape, mybir.dt.from_np(a.dtype), kind="ExternalInput").ap()
           for n, a in ins.items()]
    shapes = {"y": (P, KD, T), "kv": (P, RT, T), "kr": (DR, T), "pool": (P, PT_, 1 + NB, BUF),
              "conv": (P, FT, 1 + NB, CW - 1)}
    aps += [nc.dram_tensor("out_" + n, s, F32, kind="ExternalOutput").ap() for n, s in shapes.items()]
    program(nc, *aps)
    r = run(nc, [{"in_" + n: a for n, a in ins.items()}], core_ids=[0]).results[0]
    yy = r["out_y"].transpose(2, 1, 0).reshape(T, D)
    kv = r["out_kv"].transpose(2, 1, 0).reshape(T, R)
    kr = r["out_kr"].T
    pool = r["out_pool"].transpose(2, 3, 1, 0).reshape(1 + NB, BUF, PW)
    conv = r["out_conv"].transpose(2, 3, 1, 0).reshape(1 + NB, CW - 1, FF)
    return (yy[:NP].reshape(1, NP, D), yy[NP:].reshape(NB, NT, D),
            kv[:NP].reshape(1, 1, NP, R), kr[:NP].reshape(1, 1, NP, DR),
            kv[NP:].reshape(1, NB, NT, R), kr[NP:].reshape(1, NB, NT, DR),
            pool[:1].reshape(1, 1, BUF, PW), pool[1:].reshape(1, NB, BUF, PW),
            conv[:1].reshape(1, 1, CW - 1, FF), conv[1:].reshape(1, NB, CW - 1, FF))
```

```python
from contextlib import ExitStack

import concourse.bass as bass
from concourse import mybir

F32 = mybir.dt.float32
F32R = mybir.dt.float32r
I32 = mybir.dt.int32
ACT = mybir.ActivationFunctionType
ALU = mybir.AluOpType
AX = mybir.AxisListType

P = 128
D, NP, NB, NT = 2048, 256, 8, 8
NS = NB * NT
T = NP + NS
KD = D // P
H, DN, DR, DV, R = 16, 128, 64, 128, 512
RT = R // P
PAST, PAGE = 1024, 128
NPG = PAST // PAGE
PW, BUF = 1024, 15
PT_ = PW // P
FF, CW = 5632, 3
FT = FF // P
SCALE = float(DN + DR) ** -0.5
EPS = 1e-6
NEG = -1e30
SLAB = 16 * P
PSEG, SSEG = BUF + NP, BUF + NT
PEXT = PSEG + NB * SSEG
CPS, CSS = CW - 1 + NP, CW - 1 + NT
CEXT = CPS + NB * CSS
FPC = 4
NCH = FT // FPC

ORDER = [("ckv", 4), ("pool", 8), ("q_rope", 8), ("krope_group", 2), ("gate_b", 16), ("pool_out", 8),
         ("gate_a", 16), ("q_nope", 16), ("uk", 4), ("uv", 4), ("ukt", 4), ("sample", 2 * NB), ("uv2", 4),
         ("attn_out", 16), ("w_o", 16), ("ffn", NCH * 12)]
G0 = {}
NSLAB = 0
for _name, _n in ORDER:
    G0[_name] = NSLAB
    NSLAB += _n
GS = G0["sample"]
NDENSE = NSLAB - 2 * NB
QUAD = NPG // 2
TCOL = R + DR


def dense_index(g):
    return g if g < GS else g - 2 * NB


def split_index(g):
    return g - (4 if g > G0["ukt"] else 0) - (4 if g > G0["uv2"] else 0)


def raw_index(g):
    return dense_index(g) - (2 if g >= G0["ukt"] + 4 else 0) - (2 if g >= G0["uv2"] + 4 else 0)


NWHOLE = G0["ffn"] - split_index(G0["ffn"])
VEC = {}
NVEC = 0
for _name, _n in [("g_attn", KD), ("g_kv", RT), ("b_a", KD), ("b_b", KD), ("pool_scale", PT_), ("g_ffn", KD),
                  ("conv_w", CW * FT), ("conv_b", FT), ("g_fin", KD)]:
    VEC[_name] = NVEC
    NVEC += _n
CST = {}
NCST = 0
for _name, _n in [("cos", T), ("sin", T), ("mask", 3 * P), ("mask_new", NT), ("inv_cnt", BUF), ("ident", P),
                  ("ones", P)]:
    CST[_name] = NCST
    NCST += _n


def program(nc, slabs, x, vecs, consts, cache_t, cache, pages, pool_hist, conv_hist,
            y, kv_out, kr_out, pool_out, conv_out):
    n_phys = cache.shape[0]
    place = [nc.sbuf_base + (-nc.sbuf_base) % 64]

    def region(nbytes):
        at = place[0]
        place[0] += nbytes + (-nbytes) % 64
        assert place[0] <= nc.sbuf_usable_end, place
        return at

    def sb(name, shape, dt=F32, at=None):
        n = 4
        for d in shape[1:]:
            n *= d
        return nc.alloc_sbuf_tensor_at(name, shape, dt, offset=region(n) if at is None else at)

    with ExitStack() as ctx:
        def sem(name):
            return ctx.enter_context(nc.semaphore(name))

        t_raw = [sb(f"w_raw{s}", [P, QUAD * TCOL]) for s in range(2)]
        raw = [r[:, 0:SLAB] for r in t_raw]
        w_hi = [sb(f"w_hi{s}", [P, SLAB], F32R) for s in range(2)]
        lo_reg = [region(SLAB * 4) for s in range(2)]
        w_lo = [sb(f"w_lo{s}", [P, SLAB], F32R, at=lo_reg[s]) for s in range(2)]
        whole = raw + [sb(f"w_whole{s}", [P, SLAB], at=lo_reg[s])[:, :] for s in range(2)]
        vec = sb("vec", [P, NVEC])
        cst = sb("cst", [P, NCST])
        page_sb = sb("page_sb", [1, NB * NPG], I32)
        norm_reg = region(4096)
        rstd = sb("rstd", [P, T], at=norm_reg)
        nv = sb("norm_var", [P, T], at=norm_reg + 1280)
        na = sb("norm_tmp", [P, T], at=norm_reg + 2560)
        k_rope = [sb(f"k_rope{s}", [DR, QUAD, PAGE], at=norm_reg + 2048 * s) for s in range(2)]
        nmx = sb("neg_max", [P, 2 * H])
        rsum = sb("row_sum", [P, 2 * H])
        rinv = sb("row_inv", [P, 2 * H])
        smx = sb("sample_max", [P, NB, 12])
        ssum = sb("sample_sum", [P, NB, 4])
        TB = KD * T * 4
        a_reg = region(TB)
        b_reg = region(TB)
        r1 = region(2 * TB)
        qn_reg = region(TB)
        ol_reg = region(TB)
        ch_reg = region(2 * RT * T * 4)
        qr_reg = region(8 * T * 4)
        left = region(4096)
        c_raw = [sb("c_raw0", [P, QUAD * R], at=ch_reg), sb("c_raw1", [P, QUAD * R])]
        gate_a = sb("gate_a", [P, KD, T], at=a_reg)
        m_hi = sb("m_hi", [P, KD, T], F32R, at=a_reg)
        op_hi = sb("op_hi", [P, PT_, T], F32R, at=a_reg)
        op_lo = sb("op_lo", [P, PT_, T], F32R, at=a_reg + TB // 2)
        gate_b = sb("gate_b", [P, KD, T], at=b_reg)
        m_lo = sb("m_lo", [P, KD, T], F32R, at=b_reg)
        uext = sb("uext", [P, PT_, PEXT], at=b_reg)
        hist = sb("hist", [P, PT_ * NB, BUF], at=b_reg + PT_ * PEXT * 4)
        pstate = sb("pstate", [P, PT_, 1 + NB, BUF], at=b_reg + PT_ * PEXT * 4)
        h_hi = sb("h_hi", [P, KD, T], F32R, at=r1)
        h_lo = sb("h_lo", [P, KD, T], F32R, at=r1 + TB)
        kT = sb("kT", [P, H, NP], at=r1)
        vv = sb("vv", [P, 2, H * DV], at=r1 + 16384)
        sm = sb("sm", [P, 3, 3 * P], at=r1 + 32768)
        pt = sb("pt", [P, 2, 3 * P], at=r1 + 32768 + 4608)
        qlat = sb("qlat", [P, NB, RT, P], at=r1)
        ola = sb("ola", [P, NB, RT, P], at=r1)
        cnew = sb("cnew", [NT, NB, R], at=r1 + 16384)
        ql_hi = sb("ql_hi", [P, 2, R], F32R, at=r1 + 32768)
        ql_lo = sb("ql_lo", [P, 2, R], F32R, at=r1 + 32768 + 4096)
        xT = sb("xT", [P, KD, T], at=qn_reg)
        ta = sb("pool_ta", [P, 2, PEXT], at=qn_reg)
        tb = sb("pool_tb", [P, 2, PEXT], at=qn_reg + 4096)
        pl = sb("pooled", [P, 2, 2, T], at=qn_reg + 8192)
        op32 = sb("op32", [P, 2, T], at=qn_reg + 14336)
        qn = sb("qn", [P, H, T], at=qn_reg)
        o_hi = sb("o_hi", [P, H, T], F32R, at=qn_reg)
        x1 = sb("x1", [P, KD, T], at=qn_reg)
        sq = sb("sq", [P, KD, T], at=ol_reg)
        p_hi = sb("p_hi", [P, PT_, T], F32R, at=ol_reg)
        p_lo = sb("p_lo", [P, PT_, T], F32R, at=ol_reg + TB // 2)
        o_lo = sb("o_lo", [P, H, T], F32R, at=ol_reg)
        x_again = sb("x_again", [P, KD, T], at=ol_reg)
        c32 = sb("c32", [P, RT, T])
        kr = sb("kr", [P, T])
        c_hi = sb("c_hi", [P, RT, T], F32R, at=ch_reg)
        c_lo = sb("c_lo", [P, RT, T], F32R, at=ch_reg + RT * T * 4)
        m32 = sb("m32", [P, 2, T], at=ch_reg)
        mt = sb("m_tmp", [P, 2, T], at=ch_reg + 4096)
        qr = sb("qr", [P, 8, T], at=qr_reg)
        sp_ = sb("s_probs", [P, PAST + NT], at=qr_reg)
        spt = sb("spt", [P, PAST], at=qr_reg + 4160)
        sptn = sb("s_ptn", [NT, P], at=qr_reg + 4160 + 4096)
        qsw = sb("q_swap", [P, 2, T], at=left)
        qr_s = sb("qr_s", [DR, NB, NT, H], at=left)
        h2_hi = sb("h2_hi", [P, KD, T], F32R, at=r1)
        h2_lo = sb("h2_lo", [P, KD, T], F32R, at=r1 + TB)
        hid_hi = sb("hid_hi", [P, FPC, T], F32R, at=a_reg)
        hid_lo = sb("hid_lo", [P, FPC, T], F32R, at=a_reg + FPC * T * 4)
        aext = sb("aext", [P, 2, CEXT], at=a_reg + 2 * FPC * T * 4)
        cv = sb("cv", [P, 3, CEXT], at=a_reg + 13312)
        silu = sb("silu", [P, 2, CEXT], at=b_reg)
        hid32 = sb("hid32", [P, 2, T], at=b_reg + 4096)
        chist = sb("chist", [P, FT, NB, CW - 1], at=b_reg + 8192)
        cstate = sb("cstate", [P, FT, 1 + NB, CW - 1], at=b_reg + 12288)
        ps = ctx.enter_context(nc.psum_tensor("ps", [P, 8, 512], F32))

        def col(name, i):
            return vec[:, VEC[name] + i:VEC[name] + i + 1]

        def const(name, n=None):
            return cst[:, CST[name]:CST[name] + n]

        ident, ones = const("ident", P), const("ones", P)

        x_in = [sem(f"x_in{i}") for i in range(4)]
        vec_in, hist_in, again_in, chist_in = (sem(n) for n in ("vec_in", "hist_in", "again_in", "chist_in"))
        acc_step = [sem(f"acc_step{i}") for i in range(4)]
        raw_full = [sem("raw_full0"), sem("raw_full1")]
        hi_ready, lo_ready = sem("hi_ready"), sem("lo_ready")
        slab_used, slab_taken = sem("slab_used"), sem("slab_taken")
        sq_done, sum_done, norm, h_32, h_hi_r, h_lo_r = ([sem(f"{n}{i}") for i in range(4)] for n in
                                                         ("sq_done", "sum_done", "norm", "h_32", "h_hi_r", "h_lo_r"))
        u_zero, u_hist, st_done = sem("u_zero"), sem("u_hist"), sem("st_done")
        pool_step, pooled_r, pool_hi, pool_lo = (sem(n) for n in ("pool_step", "pooled_r", "pool_hi", "pool_lo"))
        op_32, op_hi_r, op_lo_r = sem("op_32"), sem("op_hi_r"), sem("op_lo_r")
        kr_copied, kr_step, kr_ready = sem("kr_copied"), sem("kr_step"), sem("kr_ready")
        qr_copied, qr_step, qr_ready = sem("qr_copied"), sem("qr_step"), sem("qr_ready")
        sc_done, sc_masked, mx_done, ex_done, rc_done, pn_done, pt_done, pt_taken, pv_done, ohi_done, olo_done = (
            sem("p_" + n) for n in ("sc_done", "sc_masked", "mx_done", "ex_done", "rc_done", "pn_done", "pt_done",
                                    "pt_taken", "pv_done", "ohi_done", "olo_done"))
        qrs_ready, cn_done, cn_taken = sem("qrs_ready"), sem("cn_done"), sem("cn_taken")
        t_full = [sem("t_full0"), sem("t_full1")]
        c_full, c_used = [sem("c_full0"), sem("c_full1")], sem("c_used")
        (ss_done, sn_done, sx_step, sx_done, sr_step, spn_done, spt_done, spt_act, spt_dve, spv_done, sl_done,
         ql_hi_r, ql_lo_r) = (
            sem("s_" + n) for n in ("ss_done", "sn_done", "sx_step", "sx_done", "sr_step", "spn_done", "spt_done",
                                    "spt_act", "spt_dve", "spv_done", "sl_done", "ql_hi_r", "ql_lo_r"))
        om_hi = sem("om_hi")
        whole_full = [sem("whole_full0"), sem("whole_full1")]
        mg_step, mg_32, mg_hi, mg_lo = sem("mg_step"), sem("mg_32"), sem("mg_hi"), sem("mg_lo")
        ah_ready, a_ready, cv_step, silu_r, hd_32, hd_hi, hd_lo = (
            sem("f_" + n) for n in ("ah_ready", "a_ready", "cv_step", "silu_r", "hd_32",
                                    "hd_hi", "hd_lo"))
        a_zero, cs_done, dn_done, dn_taken = sem("f_a_zero"), sem("f_cs_done"), sem("f_dn_done"), sem("f_dn_taken")
        y_step, out_sem = sem("y_step"), sem("out_sem")

        def page_halves(w, q):
            return (w[q][:, :].rearrange("p (a c) -> p a c", a=QUAD),
                    t_raw[q][:, :].rearrange("p (a c) -> p a c", a=QUAD)[:, :, 0:R])

        block = ctx.enter_context(nc.Block())

        @block.sync
        def _(sp):
            for c in range(4):
                sp.dma_start(xT[:, 4 * c:4 * c + 4, :], x[:, 4 * c:4 * c + 4, :]).then_inc(x_in[c], 16)
            sp.dma_start(raw[0], slabs[0]).then_inc(raw_full[0], 16)
            sp.dma_start(vec[:, :], vecs).then_inc(vec_in, 16)
            sp.dma_start(cst[:, :], consts).then_inc(vec_in, 16)
            sp.dma_start(page_sb[:, :], pages).then_inc(vec_in, 16)
            sp.dma_start(raw[1], slabs[1]).then_inc(raw_full[1], 16)
            sp.dma_start(hist[:, :, :], pool_hist).then_inc(hist_in, 16)

            def stream(g0, g1):
                d0 = dense_index(g0)
                with sp.Fori(d0 // 2, (d0 + g1 - g0) // 2) as i:
                    for s in range(2):
                        sp.wait_ge(lo_ready, i * 2 + (split_index(g0) - d0 + s - 1))
                        sp.dma_start(raw[s], slabs[i * 2 + s]).then_inc(raw_full[s], 16)

            stream(2, G0["ukt"])
            def pages_of(b, q):
                first = b * NPG + q * QUAD
                return nc.values_load_multi_w_load_instructions(
                    page_sb[0:1, first:first + QUAD], engines=(mybir.EngineType.SP,), min_val=0, max_val=n_phys - 1)[1]

            def whole_slabs(name, free):
                for q in range(2):
                    sp.wait_ge(slab_used, free + q + 1)
                    sp.dma_start(whole[2 + q], slabs[dense_index(G0[name] + 2 + q)]).then_inc(whole_full[q], 16)

            def into_raw(g):
                sp.dma_start(raw[g % 2], slabs[dense_index(g)]).then_inc(raw_full[g % 2], 16)

            def by_latent(b, q):
                pages4 = pages_of(b, q)
                for j in range(QUAD):
                    sp.dma_start(t_raw[q][:, j * TCOL:(j + 1) * TCOL],
                                 cache_t[bass.ds(pages4[j], 1)].rearrange("a p c -> (a p) c")).then_inc(t_full[q], 16)

            def by_token(b, q):
                if b:
                    sp.wait_ge(c_used, 2 * (b - 1) + q + 1)
                else:
                    sp.wait_ge(slab_used, G0["ukt"])
                pages4 = pages_of(b, q)
                for j in range(QUAD):
                    sp.dma_start(c_raw[q][:, j * R:(j + 1) * R],
                                 cache[bass.ds(pages4[j], 1)].rearrange("a p c -> (a p) c")).then_inc(c_full[q], 16)

            for q in range(2):
                sp.wait_ge(lo_ready, G0["ukt"] + q - 1)
                into_raw(G0["ukt"] + q)
            whole_slabs("ukt", G0["ukt"] - 2)
            for q in range(2):
                by_token(0, q)
            for q in range(2):
                sp.wait_ge(slab_used, G0["ukt"] + q + 1)
                by_latent(0, q)
            for i in range(-1, NB):
                for q in range(2):
                    if i + 2 <= NB:
                        sp.wait_ge(lo_ready, split_index(GS + 2 * (i + 1) + q) + 1)
                    if i + 2 < NB:
                        by_latent(i + 2, q)
                    elif i + 2 == NB:
                        into_raw(G0["uv2"] + q)
                if i == NB - 1:
                    whole_slabs("uv2", G0["uv2"] - 2)
                if i >= 1:
                    for q in range(2):
                        by_token(i, q)
            for q in range(2):
                sp.wait_ge(slab_used, G0["uv2"] + q + 1)
                into_raw(G0["attn_out"] + q)
            stream(G0["attn_out"] + 2, NSLAB)
            sp.wait_ge(cs_done, 2 * FT)
            sp.dma_start(conv_out, cstate[:, :, :, :]).then_inc(out_sem, 16)
            for k in range(4):
                sp.wait_ge(y_step, 4 * (k + 1))
                sp.dma_start(y[:, 4 * k:4 * k + 4, :], x1[:, 4 * k:4 * k + 4, :]).then_inc(out_sem, 16)
            sp.wait_ge(st_done, 16)
            sp.wait_ge(out_sem, 16 * 7)

        @block.gpsimd
        def _(pool):
            def halves_lo(n, lo, src, hi):
                for k in range(KD):
                    pool.wait_ge(h_hi_r[n], k + 1)
                    nc.gpsimd.tensor_tensor(lo[:, k, :], src[:, k, :], hi[:, k, :], ALU.subtract).then_inc(h_lo_r[n], 1)

            halves_lo(0, h_lo, xT, h_hi)
            pool.wait_ge(hist_in, 16)
            sample = uext[:, :, PSEG:].rearrange("p a (b t) -> p a b t", b=NB)
            hv = hist[:, :, :].rearrange("p (a b) t -> p a b t", a=PT_)
            nc.gpsimd.memset(uext[:, :, 0:BUF], 0.0).then_inc(u_zero, 1)
            for a in range(PT_):
                last = nc.gpsimd.tensor_copy(sample[:, a, :, 0:BUF], hv[:, a])
                last.then_inc(u_zero, 1)
            pool.wait_ge(u_zero, 1 + PT_)
            pool.wait_ge(slab_taken, G0["q_rope"])
            nc.gpsimd.tensor_copy(pstate[:, :, 0, :], uext[:, :, NP:NP + BUF]).then_inc(u_hist, 1)
            for half in range(2):
                a0 = half * PT_ // 2
                for a in range(a0, a0 + PT_ // 2):
                    last = nc.gpsimd.tensor_copy(pstate[:, a, 1:, :], sample[:, a, :, NT:NT + BUF])
                last.then_inc(u_hist, 1)

            pool.wait_ge(qr_ready, 2 + 8)
            pool.wait_ge(kr_ready, 1)
            for odd in range(2):
                pool.wait_ge(u_hist, 3) if odd == 0 else pool.wait_ge(qrs_ready, 1)
                for j in range(8):
                    last = nc.gpsimd.tensor_copy(qr_s[:, :, :, 2 * j + odd], qr[64 * odd:64 * odd + 64, j, NP:T]
                                                 .rearrange("p (b t) -> p b t", b=NB))
                last.then_inc(qrs_ready, 1)
            pool.wait_ge(qrs_ready, 2)
            for b in range(NB):
                pool.wait_ge(ql_hi_r, b + 1)
                nc.gpsimd.tensor_tensor(ql_lo[:, b % 2, :], qlat[:, b, :, :].rearrange("p j c -> p (j c)"),
                                        ql_hi[:, b % 2, :], ALU.subtract).then_inc(ql_lo_r, 1)
            halves_lo(2, h2_lo, sq, h2_hi)
            pool.wait_ge(chist_in, 16)
            pool.wait_ge(slab_used, G0["ffn"])
            for s in range(2):
                nc.gpsimd.memset(aext[:, s, 0:CW - 1], 0.0).then_inc(a_zero, 1)
            sa = [aext[:, s, CPS:].rearrange("p (b t) -> p b t", b=NB) for s in range(2)]

            def history(f, s):
                nc.gpsimd.tensor_copy(sa[s][:, :, 0:CW - 1], chist[:, bass.ds(f, 1), :, :].rearrange(
                    "p a b t -> p (a b) t")).then_inc(ah_ready, 1)

            def state(f, s):
                nc.gpsimd.tensor_copy(cstate[:, bass.ds(f, 1), 0, :], aext[:, s:s + 1, NP:CPS]).then_inc(cs_done, 1)
                nc.gpsimd.tensor_copy(cstate[:, bass.ds(f, 1), 1:, :].rearrange("p a b t -> p (a b) t"),
                                      sa[s][:, :, NT:CSS]).then_inc(cs_done, 1)

            for s in range(2):
                history(s, s)
            with pool.Fori(0, FT // 2 - 1) as i:
                for s in range(2):
                    pool.wait_ge(a_ready, i * 2 + (s + 1))
                    state(i * 2 + s, s)
                    pool.wait_ge(cv_step, i * 6 + 3 * (s + 1))
                    history(i * 2 + (s + 2), s)
            for s in range(2):
                pool.wait_ge(a_ready, FT - 1 + s)
                state(FT - 2 + s, s)

        @block.scalar
        def _(act):
            def copy(out, in_):
                return nc.scalar.activation(out, in_, ACT.Copy)

            def split(g):
                if 0 <= g - GS < 2 * NB:
                    act.wait_ge(t_full[g % 2], 64 * ((g - GS) // 2 + 1))
                    copy(*page_halves(w_hi, g % 2)).then_inc(hi_ready, 1)
                else:
                    act.wait_ge(raw_full[g % 2], 16 * (raw_index(g) // 2 + 1))
                    copy(w_hi[g % 2][:, :], raw[g % 2]).then_inc(hi_ready, 1)

            def steps(name, take, last=False):
                g0 = G0[name]
                n = dict(ORDER)[name]
                with act.Fori(0, n // 2) as i:
                    for s in range(2):
                        act.wait_ge(slab_used, i * 2 + (g0 + s + 1))
                        act.wait_ge(raw_full[s], i * 16 + 16 * (raw_index(g0 + 2) // 2 + 1))
                        copy(w_hi[s][:, :], raw[s]).then_inc(hi_ready, 1)
                        take(i, s)

            def split_after(g):
                act.wait_ge(slab_used, g + 1)
                split(g + 2)

            def square(n, src, k):
                nc.scalar.activation(sq[:, k, :], src[:, k, :], ACT.Square).then_inc(sq_done[n], 1)

            def root(n):
                act.wait_ge(norm[n], 1)
                nc.scalar.activation(rstd[:, :], nv[:, :], ACT.Sqrt).then_inc(norm[n], 1)

            def halves_hi(n, out, src, tiles):
                for k in range(tiles):
                    act.wait_ge(h_32[n], k + 1)
                    copy(out[:, k, :], src[:, k, :]).then_inc(h_hi_r[n], 1)

            for k in range(KD):
                if k % 4 == 0:
                    act.wait_ge(x_in[k // 4], 16)
                square(0, xT, k)
            split(0)
            root(0)
            halves_hi(0, h_hi, xT, KD)
            split(1)

            for g in range(RT):
                split_after(g)
                copy(c32[:, g, :], ps[:, g % 2, 0:T]).then_inc(slab_taken, 1)
            act.wait_ge(slab_taken, RT)
            act.wait_ge(h_lo_r[0], KD)
            for k in range(RT):
                square(1, c32, k)

            act.wait_ge(u_zero, 1 + PT_)
            for t in range(PT_):
                g = G0["pool"] + t
                split_after(g)
                copy(uext[:, t, BUF:PSEG], ps[:, g % 2, 0:NP])
                copy(uext[:, t, PSEG:].rearrange("p (b t) -> p b t", b=NB)[:, :, BUF:],
                     ps[:, g % 2, NP:T].rearrange("p (b t) -> p b t", b=NB)).then_inc(slab_taken, 1)
                if t == 1:
                    root(1)
                if t == 2:
                    halves_hi(1, c_hi, c32, RT)
                if t % 2 and t > 1:
                    j = (t - 2) // 2
                    act.wait_ge(pooled_r, j + 1)
                    copy(p_hi[:, 2 * j:2 * j + 2, :], pl[:, j % 2, :, :]).then_inc(pool_hi, 1)

            act.wait_ge(pooled_r, 4)
            copy(p_hi[:, 6:8, :], pl[:, 1, :, :]).then_inc(pool_hi, 1)

            def gate(buf, bias):
                def take(i, s):
                    k = i * 2 + s
                    nc.scalar.activation(buf[:, bass.ds(k, 1), :].rearrange("p a t -> p (a t)"), ps[:, s, 0:T],
                                         ACT.Sigmoid, bias=vec[:, bass.ds(i * 2 + (s + VEC[bias]), 1)]
                                         ).then_inc(slab_taken, 1)
                return take

            def take_rope(i, s):
                j = i * 2 + s
                act.wait_ge(qr_ready, i * 2 + (s + 1))
                copy(qr[:, bass.ds(j, 1), :].rearrange("p a t -> p (a t)"), ps[:, s, 0:T])
                for q in range(4):
                    last = copy(qsw[32 * q:32 * q + 32, s, :], ps[32 * (q ^ 1):32 * (q ^ 1) + 32, s, 0:T])
                last.then_inc(slab_taken, 1)

            steps("q_rope", take_rope)
            g = G0["krope_group"]
            split_after(g)
            act.wait_ge(qr_ready, 2 + 8)
            copy(kr[:, :], ps[:, 0, 0:T]).then_inc(kr_copied, 1)
            for q in range(4):
                last = copy(qsw[32 * q:32 * q + 32, 0, :], ps[32 * (q ^ 1):32 * (q ^ 1) + 32, 0, 0:T])
            last.then_inc(slab_taken, 1)
            split_after(g + 1)
            act.wait_ge(norm[1], 7 + RT)
            act.dma_start(kv_out, c32[:, :, :]).then_inc(out_sem, 16)
            act.wait_ge(kr_ready, 1)
            act.dma_start(kr_out, kr[0:DR, :]).then_inc(out_sem, 16)
            act.wait_ge(u_hist, 3)
            act.dma_start(pool_out, pstate[:, :, :, :]).then_inc(st_done, 16)
            for t in range(PT_):
                if t >= 2:
                    act.wait_ge(op_lo_r, t - 1)
                last = nc.scalar.activation(op32[:, t % 2, :], ps[:, t, 0:T], ACT.Copy, scale=col("pool_scale", t))
                last.then_inc(op_32, 1)
                act.wait_ge(op_32, t + 1)
                copy(op_hi[:, t, :], op32[:, t % 2, :]).then_inc(op_hi_r, 1)
            act.wait_ge(st_done, 16)

            act.wait_ge(slab_taken, G0["gate_b"])
            steps("gate_b", gate(gate_b, "b_b"))
            steps("pool_out", lambda i, s: None)
            act.wait_ge(slab_taken, G0["gate_a"])
            steps("gate_a", gate(gate_a, "b_a"))

            steps("q_nope", lambda i, s: copy(qn[:, bass.ds(i * 2 + s, 1), :].rearrange("p a t -> p (a t)"),
                                              ps[:, s, 0:T]).then_inc(slab_taken, 1))

            for j in range(4):
                g = G0["uk"] + j
                split_after(g)
                for q in range(2):
                    last = copy(kT[:, 4 * j + 2 * q:4 * j + 2 * q + 2, :].rearrange("p a t -> p (a t)"),
                                ps[:, g % 2 + 2 * q, :])
                last.then_inc(slab_taken, 1)
            for j in range(4):
                g = G0["uv"] + j
                if j < 2:
                    split_after(g)
                act.wait_ge(slab_used, g + 1)
                for q in range(2):
                    last = copy(vv[:, q, j * 512:j * 512 + 512], ps[:, g % 2 + 2 * q, :])
                last.then_inc(slab_taken, 1)
            for i in range(H + 3):
                if i < H:
                    act.wait_ge(mx_done, 2 * (i + 1))
                    for q in range(2):
                        c0, c1 = (0, P) if q == 0 else (P, 3 * P)
                        nc.scalar.activation(sm[:, i % 3, c0:c1], sm[:, i % 3, c0:c1], ACT.Exp,
                                             bias=nmx[:, 2 * i + q:2 * i + q + 1],
                                             accum_out=rsum[:, 2 * i + q:2 * i + q + 1]).then_inc(ex_done, 1)
                if 2 <= i < H + 2:
                    h = i - 2
                    act.wait_ge(pt_done, h + 1)
                    if h >= 2:
                        act.wait_ge(pv_done, h - 1)
                    copy(pt[:, h % 2, :], ps[:, 4 + h % 2, 0:3 * P]).then_inc(pt_taken, 1)
                if i >= 3:
                    h = i - 3
                    act.wait_ge(pv_done, h + 1)
                    copy(o_hi[:, h, 0:NP], ps[:, 6 + h % 2, 0:NP]).then_inc(ohi_done, 1)

            act.wait_ge(sc_done, H)
            act.wait_ge(pv_done, H)
            for b in range(NB):
                act.wait_ge(cn_done, b + 1)
                copy(cnew[:, b, :], ps[0:NT, 4 + b % 4, :]).then_inc(cn_taken, 1)

            for j in range(4):
                g = G0["ukt"] + j
                act.wait_ge(slab_used, g + 1)
                for hh in range(4):
                    src = ps[:, g % 2 + 2 * (hh // 2), (hh % 2) * 256:(hh % 2) * 256 + 256]
                    last = copy(qlat[:, :, :, :].rearrange("p b j (t h) -> p h j b t", h=H)[:, 4 * j + hh],
                                src.rearrange("p (j b t) -> p j b t", j=RT, b=NB))
                last.then_inc(slab_taken, 1)
            for q in range(2):
                split(GS + q)

            def query_hi(b):
                copy(ql_hi[:, b % 2, :], qlat[:, b, :, :].rearrange("p j c -> p (j c)")).then_inc(ql_hi_r, 1)

            act.wait_ge(slab_taken, GS)
            query_hi(0)
            for i in range(NB + 1):
                b = i - 1
                if i:
                    act.wait_ge(spt_done, i)
                    copy(spt[:, 0:PAST // 2], ps[:, 4, :])
                    copy(sptn[:, :], ps[0:NT, 7, P:2 * P]).then_inc(spt_act, 1)
                if i < NB:
                    if i + 1 < NB:
                        split_after(GS + 2 * i)
                        split_after(GS + 2 * i + 1)
                        query_hi(i + 1)
                    act.wait_ge(sx_step, 4 * (i + 1))
                    b0 = 2 * (i % 2)
                    nm = smx[:, i, 10:11]
                    nc.scalar.activation(sp_[:, 0:PAST].rearrange("p (a t) -> p a t", a=2), ps[:, b0:b0 + 2, :],
                                         ACT.Exp, bias=nm, scale=SCALE, accum_out=ssum[:, i, 0:1]).then_inc(sx_done, 1)
                    nc.scalar.activation(sp_[:, PAST:PAST + NT], smx[:, i, 1:1 + NT], ACT.Exp, bias=nm,
                                         scale=SCALE, accum_out=ssum[:, i, 1:2]).then_inc(sx_done, 1)
                if i:
                    act.wait_ge(spv_done, b + 1)
                    for j in range(RT):
                        last = copy(ola[:, b, j, :].rearrange("p (h t) -> p t h", h=H),
                                    ps[:, 6, j * P:j * P + P].rearrange("p (t h) -> p t h", h=H))
                    last.then_inc(sl_done, 1)

            for j in range(4):
                g = G0["uv2"] + j
                act.wait_ge(slab_used, g + 1)
                copy(o_hi[:, 4 * j:4 * j + 4, NP:T], ps[:, g % 2, 0:4 * NS].rearrange("p (h t) -> p h t", h=4)
                     ).then_inc(om_hi, 1)
                if j >= 2:
                    split(G0["attn_out"] + j - 2)

            def take_merged(i, s):
                act.wait_ge(mg_32, i * 2 + (s + 1))
                copy(m_hi[:, bass.ds(i * 2 + s, 1), :].rearrange("p a t -> p (a t)"), m32[:, s, :]).then_inc(mg_hi, 1)

            steps("attn_out", take_merged)
            act.wait_ge(slab_used, G0["w_o"])
            act.dma_start(x_again[:, :, :], x).then_inc(again_in, 16)

            def take_o(i, s):
                k = i * 2 + s
                act.wait_ge(slab_taken, i * 2 + (G0["w_o"] + s + 1))
                nc.scalar.activation(sq[:, bass.ds(k, 1), :], x1[:, bass.ds(k, 1), :], ACT.Square).then_inc(sq_done[2], 1)

            steps("w_o", take_o)
            act.wait_ge(slab_used, G0["ffn"])
            act.dma_start(chist[:, :, :, :], conv_hist).then_inc(chist_in, 16)

            root(2)
            halves_hi(2, h2_hi, sq, KD)

            act.wait_ge(a_zero, 2)

            def chunk(c, last_chunk):
                for l in range(12):
                    s = l % 2
                    g = c * 12 + (G0["ffn"] + l)
                    f = l // 2
                    if l < 8 and s:
                        act.wait_ge(hd_32, c * FPC + (f + 1))
                        copy(hid_hi[:, f, :], hid32[:, f % 2, :]).then_inc(hd_hi, 1)
                    if not (last_chunk and l >= 10):
                        act.wait_ge(slab_used, g + 1)
                        act.wait_ge(raw_full[s], c * 96 + 8 * (raw_index(G0["ffn"]) + l - s + 4))
                        copy(w_hi[s][:, :], raw[s]).then_inc(hi_ready, 1)
                    if last_chunk and l >= 8:
                        for k in range(4 * (l - 8), 4 * (l - 8) + 4):
                            act.wait_ge(dn_taken, 16 * NCH + k + 1)
                            square(3, x1, k)
                    if l < 8 and not s:
                        act.wait_ge(ah_ready, c * FPC + (f + 1))
                        bank = 2 * (f % 2)
                        copy(aext[:, f % 2, CW - 1:CPS], ps[:, bank, 0:NP])
                        copy(aext[:, f % 2, CPS:].rearrange("p (b t) -> p b t", b=NB)[:, :, CW - 1:],
                             ps[:, bank, NP:T].rearrange("p (b t) -> p b t", b=NB)).then_inc(a_ready, 1)
                        act.wait_ge(cv_step, c * 3 * FPC + 3 * (f + 1))
                        nc.scalar.activation(silu[:, f % 2, CW - 1:], cv[:, 2, CW - 1:], ACT.Silu,
                                             bias=vec[:, bass.ds(c * FPC + (VEC["conv_b"] + f), 1)]).then_inc(silu_r, 1)

            with act.Fori(0, NCH - 1) as c:
                chunk(c, False)
            chunk(NCH - 1, True)
            root(3)

        @block.vector
        def _(dve):
            def tt(out, a, b, op):
                return nc.vector.tensor_tensor(out, a, b, op)

            def lo_of(s):
                tt(w_lo[s][:, :], raw[s], w_hi[s][:, :], ALU.subtract).then_inc(lo_ready, 1)

            def split(g):
                dve.wait_ge(hi_ready, split_index(g) + 1)
                if 0 <= g - GS < 2 * NB:
                    for f in range(2):
                        nc.vector.tensor_copy(k_rope[g % 2][:, :, f * DR:f * DR + DR],
                                              t_raw[g % 2][f * DR:f * DR + DR, :].rearrange(
                                                  "p (a c) -> p a c", a=QUAD)[:, :, R:])
                    out, src = page_halves(w_lo, g % 2)
                    tt(out, src, page_halves(w_hi, g % 2)[0], ALU.subtract).then_inc(lo_ready, 1)
                else:
                    lo_of(g % 2)

            def acc_start(n):
                nc.vector.memset(na[:, :], 0.0).then_inc(acc_step[n], 1)

            def acc_add(n, k):
                dve.wait_ge(sq_done[n], k + 1)
                dve.wait_ge(acc_step[n], k + 1)
                tile = sq[:, k, :] if isinstance(k, int) else sq[:, bass.ds(k, 1), :].rearrange("p a t -> p (a t)")
                tt(na[:, :], na[:, :], tile, ALU.add).then_inc(acc_step[n], 1)

            def steps(name, take):
                g0 = G0[name]
                with dve.Fori(0, dict(ORDER)[name] // 2) as i:
                    for s in range(2):
                        dve.wait_ge(hi_ready, i * 2 + (split_index(g0 + 1) + s + 2))
                        lo_of(s)
                        take(i, s)

            def rsqrt(n, width):
                dve.wait_ge(sum_done[n], 1)
                nc.vector.tensor_scalar(nv[:, :], ps[:, 7, 0:T], 1.0 / width, EPS, ALU.mult,
                                        ALU.add).then_inc(norm[n], 1)
                dve.wait_ge(norm[n], 2)
                nc.vector.reciprocal(rstd[:, :], rstd[:, :]).then_inc(norm[n], 1)
                dve.wait_ge(norm[n], 3)
                tt(na[:, :], rstd[:, :], rstd[:, :], ALU.mult).then_inc(norm[n], 1)
                dve.wait_ge(norm[n], 4)
                tt(na[:, :], na[:, :], nv[:, :], ALU.mult).then_inc(norm[n], 1)
                dve.wait_ge(norm[n], 5)
                nc.vector.tensor_scalar(na[:, :], na[:, :], -0.5, 1.5, ALU.mult, ALU.add).then_inc(norm[n], 1)
                dve.wait_ge(norm[n], 6)
                tt(rstd[:, :], rstd[:, :], na[:, :], ALU.mult).then_inc(norm[n], 1)
                dve.wait_ge(norm[n], 7)

            def normed(n, out, src, gain, tiles, done):
                for k in range(tiles):
                    nc.vector.scalar_tensor_tensor(out=out[:, k, :], in0=src[:, k, :], scalar=col(gain, k),
                                                   in1=rstd[:, :], op0=ALU.mult, op1=ALU.mult).then_inc(done, 1)

            def halves_lo(n, lo, src, hi, tiles):
                for k in range(tiles):
                    dve.wait_ge(h_hi_r[n], k + 1)
                    tt(lo[:, k, :], src[:, k, :], hi[:, k, :], ALU.subtract).then_inc(h_lo_r[n], 1)

            acc_start(0)
            for k in range(KD):
                acc_add(0, k)
            split(0)
            rsqrt(0, D)
            normed(0, xT, xT, "g_attn", KD, h_32[0])
            split(1)
            for g in range(RT):
                split(g + 2)

            n_step = 0

            def pool_group(j):
                nonlocal n_step
                w = 2 << j
                dve.wait_ge(slab_taken, G0["pool"] + 2 * j + 2)
                src = uext[:, 2 * j:2 * j + 2, :]
                cur = src
                for d in range(j + 1):
                    dst = (ta, tb)[d % 2]
                    if n_step:
                        dve.wait_ge(pool_step, n_step)
                    lag = 1 << d
                    first = (2 << d) - 1
                    tt(dst[:, :, first:], cur[:, :, first:], cur[:, :, first - lag:PEXT - lag], ALU.add
                       ).then_inc(pool_step, 1)
                    n_step += 1
                    cur = dst
                dve.wait_ge(pool_step, n_step)
                if j >= 2:
                    dve.wait_ge(pool_lo, j - 1)
                    dve.wait_ge(pool_hi, j - 1)
                out = pl[:, j % 2, :, :]
                for a in range(2):
                    for lo, hi, o in ((BUF + w - 1, PSEG, w - 1),):
                        nc.vector.scalar_tensor_tensor(out=out[:, a, o:NP], in0=cur[:, a, lo:hi], scalar=1.0 / w,
                                                       in1=src[:, a, lo:hi], op0=ALU.mult, op1=ALU.subtract)
                    seg = [z[:, a, PSEG:].rearrange("p (b t) -> p b t", b=NB)[:, :, BUF:] for z in (cur, src)]
                    nc.vector.scalar_tensor_tensor(out=out[:, a, NP:T].rearrange("p (b t) -> p b t", b=NB),
                                                   in0=seg[0], scalar=1.0 / w, in1=seg[1], op0=ALU.mult,
                                                   op1=ALU.subtract)
                    last = tt(out[:, a, 0:w - 1], cur[:, a, BUF:BUF + w - 1], const("inv_cnt", w - 1), ALU.mult)
                last.then_inc(pool_step, 1)
                n_step += 1
                dve.wait_ge(pool_step, n_step)
                for a in range(2):
                    last = tt(out[:, a, 0:w - 1], out[:, a, 0:w - 1], src[:, a, BUF:BUF + w - 1], ALU.subtract)
                last.then_inc(pooled_r, 1)

            def pool_low(j):
                dve.wait_ge(pool_hi, j + 1)
                tt(p_lo[:, 2 * j:2 * j + 2, :], pl[:, j % 2, :, :], p_hi[:, 2 * j:2 * j + 2, :], ALU.subtract
                   ).then_inc(pool_lo, 1)

            for t in range(PT_):
                g = G0["pool"] + t
                split(g + 2)
                if t == 0:
                    acc_start(1)
                    for k in range(RT):
                        acc_add(1, k)
                if t == 1:
                    rsqrt(1, R)
                    normed(1, c32, c32, "g_kv", RT, h_32[1])
                if t == 2:
                    dve.wait_ge(h_32[1], RT)
                    for k in range(RT):
                        dve.wait_ge(h_hi_r[1], k + 1)
                        tt(c_lo[:, k, :], c32[:, k, :], c_hi[:, k, :], ALU.subtract).then_inc(norm[1], 1)
                if t % 2 == 0 and t:
                    if t >= 4:
                        pool_low(t // 2 - 2)
                    pool_group(t // 2 - 1)
            for s in range(2):
                nc.vector.memset(nmx[:, s:s + 1], 0.0).then_inc(qr_ready, 1)
            pool_low(2)
            pool_group(3)
            pool_low(3)

            def take_rope(i, s):
                dve.wait_ge(slab_taken, i * 2 + (G0["q_rope"] + s + 1))
                t = qr[:, bass.ds(i * 2 + s, 1), :].rearrange("p a t -> p (a t)")
                tt(t, t, const("cos", T), ALU.mult).then_inc(qr_step, 1)
                tt(qsw[:, s, :], qsw[:, s, :], const("sin", T), ALU.mult).then_inc(qr_step, 1)
                dve.wait_ge(qr_step, i * 4 + 2 * (s + 1))
                tt(t, t, qsw[:, s, :], ALU.add).then_inc(qr_ready, 1)

            steps("q_rope", take_rope)
            g = G0["krope_group"]
            split(g + 2)
            dve.wait_ge(slab_taken, g + 1)
            tt(kr[:, :], kr[:, :], const("cos", T), ALU.mult).then_inc(kr_step, 1)
            tt(qsw[:, 0, :], qsw[:, 0, :], const("sin", T), ALU.mult).then_inc(kr_step, 1)
            dve.wait_ge(kr_step, 2)
            tt(kr[:, :], kr[:, :], qsw[:, 0, :], ALU.add).then_inc(kr_ready, 1)
            split(g + 3)
            for t in range(PT_):
                dve.wait_ge(op_hi_r, t + 1)
                tt(op_lo[:, t, :], op32[:, t % 2, :], op_hi[:, t, :], ALU.subtract).then_inc(op_lo_r, 1)
            dve.wait_ge(op_lo_r, PT_)
            nc.vector.memset(nmx[:, 0:1], 0.0).then_inc(slab_taken, 1)

            steps("gate_b", lambda i, s: None)
            dve.wait_ge(slab_taken, G0["pool_out"])

            def take_pool_out(i, s):
                dve.wait_ge(slab_used, i * 2 + (G0["pool_out"] + s + 1))
                for j in range(2):
                    g = gate_b[:, bass.ds(i * 4 + (2 * s + j), 1), :].rearrange("p a t -> p (a t)")
                    last = tt(g, ps[:, s + 2 * j, 0:T], g, ALU.mult)
                last.then_inc(slab_taken, 1)

            steps("pool_out", take_pool_out)
            steps("gate_a", lambda i, s: None)
            steps("q_nope", lambda i, s: None)
            for j in range(6):
                split(G0["uk"] + 2 + j)
            for i in range(H + 4):
                if i < H:
                    dve.wait_ge(sc_done, i + 1)
                    if i >= 3:
                        dve.wait_ge(pt_done, i - 2)
                    nc.vector.scalar_tensor_tensor(out=sm[:, i % 3, :], in0=ps[:, 2 + i % 2, 0:3 * P], scalar=SCALE,
                                                   in1=const("mask", 3 * P), op0=ALU.mult, op1=ALU.add
                                                   ).then_inc(sc_masked, 1)
                    dve.wait_ge(sc_masked, i + 1)
                    for q in range(2):
                        c0, c1 = (0, P) if q == 0 else (P, 3 * P)
                        nc.vector.tensor_reduce(nmx[:, 2 * i + q:2 * i + q + 1], sm[:, i % 3, c0:c1], AX.X, ALU.max,
                                                negate=True).then_inc(mx_done, 1)
                if 1 <= i < H + 1:
                    h = i - 1
                    dve.wait_ge(ex_done, 2 * (h + 1))
                    nc.vector.reciprocal(rinv[:, 2 * h:2 * h + 2], rsum[:, 2 * h:2 * h + 2]).then_inc(rc_done, 1)
                    dve.wait_ge(rc_done, h + 1)
                    for q in range(2):
                        c0, c1 = (0, P) if q == 0 else (P, 3 * P)
                        nc.vector.tensor_scalar(sm[:, h % 3, c0:c1], sm[:, h % 3, c0:c1],
                                                rinv[:, 2 * h + q:2 * h + q + 1], None, ALU.mult).then_inc(pn_done, 1)
                if i >= 4:
                    h = i - 4
                    dve.wait_ge(ohi_done, h + 1)
                    tt(o_lo[:, h, 0:NP], ps[:, 6 + h % 2, 0:NP], o_hi[:, h, 0:NP], ALU.subtract).then_inc(olo_done, 1)

            for q in range(2):
                dve.wait_ge(slab_used, G0["ukt"] + 2 + q + 1)
                split(GS + q)

            for i in range(NB + 1):
                if i:
                    dve.wait_ge(spt_done, i)
                    nc.vector.tensor_copy(spt[:, PAST // 2:], ps[:, 5, :]).then_inc(spt_dve, 1)
                if i < NB:
                    if i + 1 < NB:
                        split(GS + 2 * (i + 1))
                    dve.wait_ge(ss_done, i + 1)
                    tt(smx[:, i, 1:1 + NT], ps[:, 7, 0:NT], const("mask_new", NT), ALU.add).then_inc(sn_done, 1)
                    b0 = 2 * (i % 2)
                    nc.vector.tensor_reduce(smx[:, i, 0:1], ps[:, b0:b0 + 2, :], AX.XY, ALU.max).then_inc(sx_step, 1)
                    dve.wait_ge(sx_step, 4 * i + 1)
                    dve.wait_ge(sn_done, i + 1)
                    nc.vector.tensor_reduce(smx[:, i, 9:10], smx[:, i, 0:1 + NT], AX.X, ALU.max).then_inc(sx_step, 1)
                    dve.wait_ge(sx_step, 4 * i + 2)
                    nc.vector.tensor_scalar(smx[:, i, 10:11], smx[:, i, 9:10], -SCALE, None, ALU.mult
                                            ).then_inc(sx_step, 2)
                    if i + 1 < NB:
                        split(GS + 2 * (i + 1) + 1)
                    dve.wait_ge(sx_done, 2 * (i + 1))
                    tt(ssum[:, i, 2:3], ssum[:, i, 0:1], ssum[:, i, 1:2], ALU.add).then_inc(sr_step, 1)
                    dve.wait_ge(sr_step, 2 * i + 1)
                    nc.vector.reciprocal(ssum[:, i, 3:4], ssum[:, i, 2:3]).then_inc(sr_step, 1)
                    dve.wait_ge(sr_step, 2 * i + 2)
                    nc.vector.tensor_scalar(sp_[:, :], sp_[:, :], ssum[:, i, 3:4], None, ALU.mult).then_inc(spn_done, 1)
            nc.vector.memset(nmx[:, 0:1], 0.0).then_inc(slab_taken, 2 * NB)

            for j in range(4):
                g = G0["uv2"] + j
                dve.wait_ge(om_hi, j + 1)
                tt(o_lo[:, 4 * j:4 * j + 4, NP:T], ps[:, g % 2, 0:4 * NS].rearrange("p (h t) -> p h t", h=4),
                   o_hi[:, 4 * j:4 * j + 4, NP:T], ALU.subtract).then_inc(slab_taken, 1)
                if j >= 2:
                    split(G0["attn_out"] + j - 2)

            def take_merged(i, s):
                k = i * 2 + s
                dve.wait_ge(slab_used, i * 2 + (G0["attn_out"] + s + 1))
                tt(mt[:, s, :], ps[:, s, 0:T], gate_a[:, bass.ds(k, 1), :].rearrange("p a t -> p (a t)"), ALU.mult
                   ).then_inc(slab_taken, 1)
                dve.wait_ge(slab_taken, i * 2 + (G0["attn_out"] + s + 1))
                tt(m32[:, s, :], mt[:, s, :], gate_b[:, bass.ds(k, 1), :].rearrange("p a t -> p (a t)"), ALU.add
                   ).then_inc(mg_32, 1)
                dve.wait_ge(mg_hi, i * 2 + (s + 1))
                tt(m_lo[:, bass.ds(k, 1), :].rearrange("p a t -> p (a t)"), m32[:, s, :],
                   m_hi[:, bass.ds(k, 1), :].rearrange("p a t -> p (a t)"), ALU.subtract).then_inc(mg_lo, 1)

            steps("attn_out", take_merged)
            dve.wait_ge(again_in, 16)

            def take_o(i, s):
                k = i * 2 + s
                dve.wait_ge(slab_used, i * 2 + (G0["w_o"] + s + 1))
                tt(x1[:, bass.ds(k, 1), :].rearrange("p a t -> p (a t)"), ps[:, s, 0:T],
                   x_again[:, bass.ds(k, 1), :].rearrange("p a t -> p (a t)"), ALU.add).then_inc(slab_taken, 1)
                acc_add(2, k)

            acc_start(2)
            steps("w_o", take_o)
            rsqrt(2, D)
            normed(2, sq, x1, "g_ffn", KD, h_32[2])

            nc.vector.memset(nmx[:, 1:2], 0.0).then_inc(dn_taken, 16)

            def chunk(c, last_chunk):
                for l in range(12):
                    s = l % 2
                    f = l // 2
                    g = c * 12 + (G0["ffn"] + l)
                    if l < 8 and s:
                        vb = 2 * (f % 2) + 1
                        dve.wait_ge(slab_used, g + 1)
                        dve.wait_ge(silu_r, c * FPC + (f + 1))
                        nc.vector.tensor_tensor(hid32[:, f % 2, 0:NP], ps[:, vb, 0:NP], silu[:, f % 2, CW - 1:CPS],
                                                ALU.mult)
                        tt(hid32[:, f % 2, NP:T].rearrange("p (b t) -> p b t", b=NB),
                           ps[:, vb, NP:T].rearrange("p (b t) -> p b t", b=NB),
                           silu[:, f % 2, CPS:].rearrange("p (b t) -> p b t", b=NB)[:, :, CW - 1:],
                           ALU.mult).then_inc(hd_32, 1)
                        dve.wait_ge(hd_32, c * FPC + (f + 1))
                        dve.wait_ge(hd_hi, c * FPC + (f + 1))
                        tt(hid_lo[:, f, :], hid32[:, f % 2, :], hid_hi[:, f, :], ALU.subtract).then_inc(hd_lo, 1)
                    if l >= 8:
                        for n in range(4):
                            bank = 4 * (1 - s) + n
                            k = 4 * (l - 8) + n
                            if n < 3:
                                dve.wait_ge(dn_done, c * 12 + (3 * (l - 8) + n + 1))
                            else:
                                dve.wait_ge(slab_used, g + 1)
                            tt(x1[:, k, :], ps[:, bank, 0:T], x1[:, k, :], ALU.add).then_inc(dn_taken, 1)
                        if last_chunk:
                            for k in range(4 * (l - 8), 4 * (l - 8) + 4):
                                acc_add(3, k)
                    if not (last_chunk and l >= 10):
                        dve.wait_ge(hi_ready, g + (3 - NWHOLE))
                        lo_of(s)
                    if l < 8 and not s:
                        dve.wait_ge(a_ready, c * FPC + (f + 1))
                        dve.wait_ge(ah_ready, c * FPC + (f + 1))
                        a = aext[:, f % 2, :]
                        for j in range(CW):
                            w = vec[:, bass.ds(c * FPC + (VEC["conv_w"] + j * FT + f), 1)]
                            src = a[:, j:CEXT - (CW - 1 - j)]
                            dst = cv[:, j, CW - 1:]
                            if j == 0:
                                nc.vector.tensor_scalar(dst, src, w, None, ALU.mult).then_inc(cv_step, 1)
                            else:
                                dve.wait_ge(cv_step, c * 3 * FPC + (3 * f + j))
                                nc.vector.scalar_tensor_tensor(out=dst, in0=src, scalar=w, in1=cv[:, j - 1, CW - 1:],
                                                               op0=ALU.mult, op1=ALU.add).then_inc(cv_step, 1)

            with dve.Fori(0, NCH - 1) as c:
                chunk(c, False)
            acc_start(3)
            chunk(NCH - 1, True)
            rsqrt(3, D)
            for k in range(KD):
                nc.vector.scalar_tensor_tensor(out=x1[:, k, :], in0=x1[:, k, :], scalar=col("g_fin", k),
                                               in1=rstd[:, :], op0=ALU.mult, op1=ALU.mult).then_inc(y_step, 1)

        @block.tensor
        def _(pe):
            def mm(out, a, b, start, stop, **kw):
                return nc.tensor.matmul(out, a, b, start=start, stop=stop, **kw)

            def blk(w, n, m=1):
                return w[:, n * P:(n + m) * P]

            def slab(s, g, outs, per_out=False, before=None, free=True, whole_before=0):
                pe.wait_ge(hi_ready, g + (1 - whole_before))
                if free:
                    pe.wait_ge(slab_taken, g - 1)
                if per_out:
                    pe.wait_ge(lo_ready, g + (1 - whole_before))

                def high(out, terms):
                    for k, (w, hi, lo) in enumerate(terms):
                        if before is not None:
                            before(k)
                        mm(out, w(w_hi[s]), hi, k == 0, False)
                        mm(out, w(w_hi[s]), lo, False, False)

                def low(out, terms):
                    for k, (w, hi, lo) in enumerate(terms):
                        last = mm(out, w(w_lo[s]), hi, False, k == len(terms) - 1)
                    return last

                if per_out:
                    for out, terms in outs:
                        high(out, terms)
                        last = low(out, terms)
                else:
                    for out, terms in outs:
                        high(out, terms)
                    pe.wait_ge(lo_ready, g + (1 - whole_before))
                    for out, terms in outs:
                        last = low(out, terms)
                last.then_inc(slab_used, 1)

            def wb(n, m=1):
                return lambda w: blk(w, n, m)

            def dense(s, hi, lo):
                return [(ps[:, s, 0:T], [(wb(k), hi[:, k, :], lo[:, k, :]) for k in range(KD)])]

            def group(name, outs_of, before=None, **kw):
                g0 = G0[name]
                kw["whole_before"] = g0 - split_index(g0)
                if before is not None:
                    slab(0, g0, outs_of(0), before=before, **kw)
                    slab(1, g0 + 1, outs_of(1), **kw)
                with pe.Fori(0 if before is None else 1, dict(ORDER)[name] // 2) as i:
                    for s in range(2):
                        slab(s, i * 2 + (g0 + s), outs_of(s), **kw)

            def sum_squares(n, tiles):
                pe.wait_ge(acc_step[n], tiles + 1)
                mm(ps[:, 7, 0:T], ones, na[:, :], True, True).then_inc(sum_done[n], 1)

            pe.wait_ge(vec_in, 48)
            sum_squares(0, KD)

            def wait_h(n):
                def before(k):
                    pe.wait_ge(h_hi_r[n], k + 1)
                    pe.wait_ge(h_lo_r[n], k + 1)
                return before

            slab(0, 0, dense(0, h_hi, h_lo), before=wait_h(0), free=False)
            slab(1, 1, dense(1, h_hi, h_lo), free=False)
            for g in range(2, RT):
                slab(g % 2, g, dense(g % 2, h_hi, h_lo))
            g = G0["pool"]
            slab(0, g, dense(0, h_hi, h_lo))
            sum_squares(1, RT)
            slab(1, g + 1, dense(1, h_hi, h_lo))
            with pe.Fori(1, PT_ // 2) as i:
                for s in range(2):
                    slab(s, i * 2 + (g + s), dense(s, h_hi, h_lo))
            group("q_rope", lambda s: dense(s, h_hi, h_lo))
            g = G0["krope_group"]
            slab(0, g, dense(0, h_hi, h_lo))
            pe.wait_ge(norm[1], 1)
            pe.wait_ge(pool_hi, 4)
            pe.wait_ge(pool_lo, 4)
            pe.wait_ge(hi_ready, g + 2)
            pe.wait_ge(lo_ready, g + 2)
            pe.wait_ge(slab_taken, g)
            for t in (1, 2, 3, 4, 5, 6, 7, 0):
                if t == 0:
                    pe.wait_ge(slab_taken, g + 1)
                for k in range(2):
                    j = 2 * (t // 2) + k
                    mm(ps[:, t, 0:T], blk(w_hi[1], 2 * t + k), p_hi[:, j, :], k == 0, False)
                    mm(ps[:, t, 0:T], blk(w_hi[1], 2 * t + k), p_lo[:, j, :], False, False)
                    last = mm(ps[:, t, 0:T], blk(w_lo[1], 2 * t + k), p_hi[:, j, :], False, k == 1)
            last.then_inc(slab_used, 1)
            pe.wait_ge(op_32, 2)
            group("gate_b", lambda s: dense(s, h_hi, h_lo))
            group("pool_out", lambda s: [(ps[:, s + 2 * j, 0:T], [(wb(8 * j + k), op_hi[:, k, :], op_lo[:, k, :])
                                                                  for k in range(PT_)]) for j in range(2)])
            for name in ("gate_a", "q_nope"):
                group(name, lambda s: dense(s, h_hi, h_lo))

            for j in range(4):
                g = G0["uk"] + j
                slab(g % 2, g, [(ps[:, g % 2 + 2 * (hh // 2), (hh % 2) * NP:(hh % 2) * NP + NP],
                                 [(wb(4 * hh + r), c_hi[:, r, 0:NP], c_lo[:, r, 0:NP]) for r in range(RT)])
                                for hh in range(4)], per_out=True)
            for j in range(4):
                g = G0["uv"] + j
                s = g % 2
                pe.wait_ge(hi_ready, g + 1)
                pe.wait_ge(lo_ready, g + 1)
                pe.wait_ge(slab_taken, g - 1)
                for q in range(2):
                    for r in range(RT):
                        ch, cl = c_hi[:, r, q * P:q * P + P], c_lo[:, r, q * P:q * P + P]
                        mm(ps[:, s + 2 * q, :], ch, blk(w_hi[s], 4 * r, 4), r == 0, False)
                        mm(ps[:, s + 2 * q, :], cl, blk(w_hi[s], 4 * r, 4), False, False)
                        last = mm(ps[:, s + 2 * q, :], ch, blk(w_lo[s], 4 * r, 4), False, r == RT - 1)
                last.then_inc(slab_used, 1)

            pe.wait_ge(slab_taken, G0["ukt"])
            pe.wait_ge(kr_ready, 1)
            for i in range(H + 3):
                if i < H:
                    if i >= 2:
                        pe.wait_ge(sc_masked, i - 1)
                    r0 = 64 * (i % 2)
                    for q in range(2):
                        out = ps[:, 2 + i % 2, q * P:q * P + (q + 1) * P]
                        mm(out, qn[:, i, q * P:q * P + P], kT[:, i, 0:(q + 1) * P], True, False)
                        last = mm(out, qr[r0:r0 + 64, i // 2, q * P:q * P + P], kr[r0:r0 + 64, 0:(q + 1) * P],
                                  False, True)
                    last.then_inc(sc_done, 1)
                if 2 <= i < H + 2:
                    h = i - 2
                    pe.wait_ge(pn_done, 2 * (h + 1))
                    if h >= 2:
                        pe.wait_ge(pt_taken, h - 1)
                    for q in range(3):
                        last = nc.tensor.transpose(ps[:, 4 + h % 2, q * P:q * P + P], sm[:, h % 3, q * P:q * P + P],
                                                   ident)
                    last.then_inc(pt_done, 1)
                if i >= 3:
                    h = i - 3
                    pe.wait_ge(pt_taken, h + 1)
                    if h >= 2:
                        pe.wait_ge(olo_done, h - 1)
                    out = ps[:, 6 + h % 2, :]
                    mm(out[:, 0:NP], vv[:, 0, h * DV:(h + 1) * DV], pt[:, h % 2, 0:NP], True, False)
                    mm(out[:, P:NP], vv[:, 1, h * DV:(h + 1) * DV], pt[:, h % 2, NP:3 * P], False, True
                       ).then_inc(pv_done, 1)

            for b in range(NB):
                if b < 4:
                    pe.wait_ge(olo_done, H)
                else:
                    pe.wait_ge(cn_taken, b - 3)
                for r in range(RT):
                    last = nc.tensor.transpose(ps[0:NT, 4 + b % 4, r * P:r * P + P],
                                               c32[:, r, NP + NT * b:NP + NT * (b + 1)], ident)
                last.then_inc(cn_done, 1)
            pe.wait_ge(sc_masked, H)

            def slab_ready(g, j, nth):
                if j < 2:
                    pe.wait_ge(raw_full[j], 16 * (raw_index(g) // 2 + 1))
                else:
                    pe.wait_ge(whole_full[j % 2], 16 * nth)
                pe.wait_ge(slab_taken, g - 1)

            for j in range(4):
                g = G0["ukt"] + j
                slab_ready(g, j, 1)
                for hh in range(4):
                    for r in range(RT):
                        c0 = (hh % 2) * 256 + r * NS
                        last = mm(ps[:, g % 2 + 2 * (hh // 2), c0:c0 + NS], blk(whole[j], 4 * hh + r),
                                  qn[:, 4 * j + hh, NP:T], True, True)
                last.then_inc(slab_used, 1)
            pe.wait_ge(cn_taken, NB)
            pe.wait_ge(qrs_ready, 2)
            pe.wait_ge(slab_taken, GS)

            def score(b, q):
                s = q
                g = GS + 2 * b + q
                out = ps[:, 2 * (b % 2) + q, :]
                hi, lo = ([w[s][:, :].rearrange("p (a j c) -> p j a c", a=QUAD, j=RT)[:, r] for r in range(RT)]
                          for w in (w_hi, w_lo))
                o3 = out.rearrange("p (a c) -> p a c", a=QUAD)
                pe.wait_ge(hi_ready, split_index(g) + 1)
                pe.wait_ge(ql_lo_r, b + 1)
                for r in range(RT):
                    mm(o3, ql_hi[:, b % 2, r * P:(r + 1) * P], hi[r], r == 0, False)
                    mm(o3, ql_lo[:, b % 2, r * P:(r + 1) * P], hi[r], False, False)
                pe.wait_ge(lo_ready, split_index(g) + 1)
                for r in range(RT):
                    mm(o3, ql_hi[:, b % 2, r * P:(r + 1) * P], lo[r], False, False)
                mm(out, qr_s[:, b, :, :].rearrange("p t h -> p (t h)"), k_rope[q][:, :, :].rearrange("p a t -> p (a t)"),
                   False, True).then_inc(slab_used, 1)

            def values(b, q):
                pe.wait_ge(c_full[q], 64 * (b + 1))
                for a in range(QUAD):
                    pg = q * QUAD + a
                    for r in range(RT):
                        last = mm(ps[:, 6, r * P:r * P + P], c_raw[q][:, a * R + r * P:a * R + r * P + P],
                                  spt[:, pg * P:pg * P + P], pg == 0 and r == 0, False, skip_group_check=True)
                last.then_inc(c_used, 1)

            for i in range(NB + 1):
                b = i - 1
                if i < NB:
                    if i >= 2:
                        pe.wait_ge(sx_done, 2 * (i - 1))
                    score(i, 0)
                if i:
                    pe.wait_ge(spn_done, b + 1)
                    for pg in range(NPG):
                        nc.tensor.transpose(ps[:, 4 + pg // 4, (pg % 4) * P:(pg % 4 + 1) * P],
                                            sp_[:, pg * P:pg * P + P], ident)
                    nc.tensor.transpose(ps[0:NT, 7, P:2 * P], sp_[:, PAST:PAST + NT], ident).then_inc(spt_done, 1)
                if i < NB:
                    score(i, 1)
                    out = ps[:, 7, 0:NT]
                    if i:
                        pe.wait_ge(spt_act, i)
                    t0 = NP + NT * i
                    for r in range(RT):
                        mm(out, qlat[:, i, r, :], c32[:, r, t0:t0 + NT], r == 0, False)
                    mm(out, qr_s[0:DR, i, :, :].rearrange("p t h -> p (t h)"), kr[0:DR, t0:t0 + NT], False, True
                       ).then_inc(ss_done, 1)
                if i:
                    pe.wait_ge(spt_act, b + 1)
                    pe.wait_ge(spt_dve, b + 1)
                    if b:
                        pe.wait_ge(sl_done, b)
                    values(b, 0)
                    values(b, 1)
                    for r in range(RT):
                        last = mm(ps[:, 6, r * P:r * P + P], cnew[:, b, r * P:r * P + P], sptn[:, :], False,
                                  r == RT - 1, skip_group_check=True)
                    last.then_inc(spv_done, 1)

            pe.wait_ge(sl_done, NB)
            for j in range(4):
                g = G0["uv2"] + j
                slab_ready(g, j, 2)
                for hh in range(4):
                    for r in range(RT):
                        last = mm(ps[:, g % 2, hh * NS:(hh + 1) * NS].rearrange("p (b t) -> p b t", b=NB),
                                  blk(whole[j], 4 * r + hh), ola[:, :, r, (4 * j + hh) * NT:(4 * j + hh + 1) * NT],
                                  r == 0, r == RT - 1)
                last.then_inc(slab_used, 1)
            group("attn_out", lambda s: dense(s, o_hi, o_lo),
                  before=lambda k: pe.wait_ge(slab_taken, G0["uv2"] + k // 4 + 1))
            group("w_o", lambda s: dense(s, m_hi, m_lo), before=lambda k: pe.wait_ge(mg_lo, k + 1))
            sum_squares(2, KD)
            pe.wait_ge(norm[2], 1)
            pe.wait_ge(dn_taken, 16)

            with pe.Fori(0, NCH) as c:
                for l in range(8):
                    s, f = l % 2, l // 2
                    if s == 0:
                        if f >= 2:
                            pe.wait_ge(a_ready, c * FPC + (f - 1))
                    elif f >= 2:
                        pe.wait_ge(hd_32, c * FPC + (f - 1))
                    if l == 0:
                        pe.wait_ge(dn_taken, c * 16 + 16)
                    slab(s, c * 12 + (G0["ffn"] + l),
                         [(ps[:, 2 * (f % 2) + s, 0:T], [(wb(k), h2_hi[:, k, :], h2_lo[:, k, :]) for k in range(KD)])],
                         free=False, before=wait_h(2) if l == 0 else None, whole_before=NWHOLE)
                for d in range(4):
                    s = d % 2
                    g = c * 12 + (G0["ffn"] + 8 + d)
                    pe.wait_ge(hi_ready, g + (1 - NWHOLE))
                    pe.wait_ge(lo_ready, g + (1 - NWHOLE))
                    banks = [4 * (1 - s) + n for n in range(4)]
                    order = ([(n, k) for k in range(FPC) for n in range(4)] if d == 0 else
                             [(n, k) for n in range(4) for k in range(FPC)])
                    for n, k in order:
                        if d == 0 and n == 0:
                            pe.wait_ge(hd_hi, c * FPC + (k + 1))
                            pe.wait_ge(hd_lo, c * FPC + (k + 1))
                        if d >= 2 and k == 0:
                            pe.wait_ge(dn_taken, c * 16 + (16 + 4 * (d - 2) + n + 1))
                        out = ps[:, banks[n], 0:T]
                        w = 4 * n + k
                        mm(out, blk(w_hi[s], w), hid_hi[:, k, :], k == 0, False)
                        mm(out, blk(w_hi[s], w), hid_lo[:, k, :], False, False)
                        last = mm(out, blk(w_lo[s], w), hid_hi[:, k, :], False, k == FPC - 1)
                        if k == FPC - 1:
                            last.then_inc(dn_done if n < 3 else slab_used, 1)
            sum_squares(3, KD)


def _tables():
    import numpy as np

    t = np.zeros((P, NCST), np.float32)
    half = DR // 2
    inv = (np.float32(10000.0) ** (-np.arange(half, dtype=np.float32) / np.float32(half))).astype(np.float32)
    pos = np.concatenate([np.arange(NP), np.tile(PAST + np.arange(NT), NB)]).astype(np.float32)
    ang = (pos[None, :] * inv[:, None]).astype(np.float32).astype(np.float64)
    t[:, CST["cos"]:CST["cos"] + T] = np.tile(np.cos(ang), (4, 1))
    t[:, CST["sin"]:CST["sin"] + T] = np.concatenate([-np.sin(ang), np.sin(ang)] * 2)
    tri = np.where(np.arange(P)[None, :] <= np.arange(P)[:, None], 0.0, NEG)
    t[:, CST["mask"]:CST["mask"] + P] = tri
    t[:, CST["mask"] + 2 * P:CST["mask"] + 3 * P] = tri
    t[:, CST["mask_new"]:CST["mask_new"] + NT] = np.where(np.arange(NT)[None, :] <= (np.arange(P) // H)[:, None],
                                                          0.0, NEG)
    t[:, CST["inv_cnt"]:CST["inv_cnt"] + BUF] = 1.0 / np.arange(1, BUF + 1)
    t[:, CST["ident"]:CST["ident"] + P] = np.eye(P)
    t[:, CST["ones"]:CST["ones"] + P] = 1.0
    return t


def _slabs(w_in, w_uk, w_uv, w_attn_out, w_pool_group, w_pool_out, w_o, w_up, w_down):
    import numpy as np

    out = np.empty((NDENSE, P, 16, P), np.float32)

    def put(name, blocks, off=0):
        g = dense_index(G0[name]) + off
        out[g:g + len(blocks)] = blocks.transpose(0, 2, 1, 3)

    def tiles(w):
        return w.reshape(w.shape[0] // P, P, w.shape[1] // P, P).transpose(2, 0, 1, 3)

    qc = H * (DN + DR)
    q = w_in[:, :qc].reshape(D, H, DN + DR)
    put("q_nope", tiles(q[:, :, :DN].reshape(D, H * DN)))
    put("q_rope", tiles(q[:, :, DN:].reshape(D, H * DR)))
    put("ckv", tiles(w_in[:, qc:qc + R]))
    k = w_in[:, qc + R:qc + R + DR]
    put("krope_group", tiles(np.concatenate([k, k], 1)))
    c = qc + R + DR
    put("pool", tiles(w_in[:, c:c + PW]))
    put("gate_a", tiles(w_in[:, c + PW:c + PW + D]))
    put("gate_b", tiles(w_in[:, c + PW + D:]))
    g = w_pool_group.reshape(4, 2, P, 2, P).transpose(0, 3, 1, 2, 4)
    put("krope_group", g.reshape(1, 16, P, P), 1)
    put("pool_out", tiles(w_pool_out).reshape(8, 16, P, P))
    uk = w_uk.reshape(RT, P, 4, 4, DN)
    put("uk", uk.transpose(2, 3, 0, 1, 4).reshape(4, 16, P, P))
    put("ukt", uk.transpose(2, 3, 0, 4, 1).reshape(4, 16, P, P))
    uv = w_uv.reshape(RT, P, 4, 4, DV).transpose(2, 0, 3, 1, 4).reshape(4, 16, P, P)
    put("uv", uv)
    put("uv2", uv)
    put("attn_out", tiles(w_attn_out))
    put("w_o", tiles(w_o))
    up = tiles(w_up).reshape(2, NCH, FPC, KD, P, P).transpose(1, 2, 0, 3, 4, 5).reshape(NCH, 8, 16, P, P)
    down = w_down.reshape(NCH, FPC, P, 4, 4, P).transpose(0, 3, 4, 1, 2, 5).reshape(NCH, 4, 16, P, P)
    put("ffn", np.concatenate([up, down], 1).reshape(NCH * 12, 16, P, P))
    return out.reshape(NDENSE, P, SLAB)


def kernel(x_prompt, x_sample, cache_kv_latent, cache_k_rope, page_table, state_pool, state_conv, norm_attn_g, w_in,
           b_gates, kv_norm_g, w_uk, w_uv, w_attn_out, w_pool_group, pool_scale, w_pool_out, w_o, norm_ffn_g, w_up,
           conv_w, conv_b, w_down, norm_final_g):
    import numpy as np
    import concourse.bacc as bacc
    from concourse.bass_utils import run_bass_kernel_spmd as run

    def arr(a):
        return np.asarray(a)

    def cols(*vs):
        return np.concatenate([arr(v).reshape(-1, P).T for v in vs], 1)

    nc = bacc.Bacc("TRN2", target_bir_lowering=False, num_devices=1, dynamic_dma_scratch_size=1024)
    xx = np.concatenate([arr(x_prompt).reshape(NP, D), arr(x_sample).reshape(NS, D)])
    cache = arr(cache_kv_latent)[0]
    ins = {
        "slabs": _slabs(arr(w_in)[0], arr(w_uk)[0], arr(w_uv)[0], arr(w_attn_out)[0], arr(w_pool_group)[0],
                        arr(w_pool_out)[0], arr(w_o)[0], arr(w_up)[0], arr(w_down)[0]),
        "x": xx.T.reshape(KD, P, T).transpose(1, 0, 2),
        "vecs": cols(norm_attn_g, kv_norm_g, arr(b_gates)[0, 0], arr(b_gates)[0, 1], pool_scale, norm_ffn_g,
                     conv_w, conv_b, norm_final_g),
        "consts": _tables(),
        "cache_t": np.concatenate(
            [cache.reshape(-1, PAGE, RT, P).transpose(0, 3, 2, 1).reshape(-1, P, RT * PAGE),
             arr(cache_k_rope)[0].reshape(-1, 2, PAGE // 2, DR).transpose(0, 1, 3, 2).reshape(-1, P, PAGE // 2)], 2),
        "cache": cache,
        "pages": arr(page_table).reshape(1, -1),
        "pool_hist": arr(state_pool)[0].reshape(NB, BUF, PT_, P).transpose(3, 2, 0, 1).reshape(P, PT_ * NB, BUF),
        "conv_hist": arr(state_conv)[0].reshape(NB, CW - 1, FT, P).transpose(3, 2, 0, 1),
    }
    ins = {n: np.ascontiguousarray(a) for n, a in ins.items()}
    aps = [nc.dram_tensor("in_" + n, a.shape, mybir.dt.from_np(a.dtype), kind="ExternalInput").ap()
           for n, a in ins.items()]
    shapes = {"y": (P, KD, T), "kv": (P, RT, T), "kr": (DR, T), "pool": (P, PT_, 1 + NB, BUF),
              "conv": (P, FT, 1 + NB, CW - 1)}
    aps += [nc.dram_tensor("out_" + n, s, F32, kind="ExternalOutput").ap() for n, s in shapes.items()]
    program(nc, *aps)
    r = run(nc, [{"in_" + n: a for n, a in ins.items()}], core_ids=[0]).results[0]
    yy = r["out_y"].transpose(2, 1, 0).reshape(T, D)
    kv = r["out_kv"].transpose(2, 1, 0).reshape(T, R)
    kr = r["out_kr"].T
    pool = r["out_pool"].transpose(2, 3, 1, 0).reshape(1 + NB, BUF, PW)
    conv = r["out_conv"].transpose(2, 3, 1, 0).reshape(1 + NB, CW - 1, FF)
    return (yy[:NP].reshape(1, NP, D), yy[NP:].reshape(NB, NT, D),
            kv[:NP].reshape(1, 1, NP, R), kr[:NP].reshape(1, 1, NP, DR),
            kv[NP:].reshape(1, NB, NT, R), kr[NP:].reshape(1, NB, NT, DR),
            pool[:1].reshape(1, 1, BUF, PW), pool[1:].reshape(1, NB, BUF, PW),
            conv[:1].reshape(1, 1, CW - 1, FF), conv[1:].reshape(1, NB, CW - 1, FF))
```
